# Optimizing a Trainium2 kernel written in Bass

```python
import math
import jax
import jax.numpy as jnp
from jax import lax
import numpy as np

D_MODEL = 1024
BATCH = 1
SEQ = 1024
DEPTH = 2
DEC_BATCH = 8
DEC_SEQ = 8
PAST_LEN = 1024
PAGE_SIZE = 128

N_EVEN = (DEPTH + 1) // 2
N_ODD = DEPTH // 2
PLE_DIM = 256
D_FF = 4 * D_MODEL
HG_WIDTH = D_MODEL // 2
HG_HEADS = 4
HG_DK = HG_WIDTH // HG_HEADS
HG_DV = HG_DK
HG_CHUNK = 64
DA_WIDTH = D_MODEL - HG_WIDTH
DA_HEADS = 4
DA_DV = DA_WIDTH // DA_HEADS
DA_DH = DA_DV // 2
DA_QK = DA_HEADS * 2 * DA_DH
Q_BLOCK = 128
IN_SPLITS = [HG_WIDTH, 2 * HG_WIDTH, 3 * HG_WIDTH, 4 * HG_WIDTH,
             4 * HG_WIDTH + DA_QK, 4 * HG_WIDTH + 2 * DA_QK]
IN_COLS = 4 * HG_WIDTH + 2 * DA_QK + DA_WIDTH
RW_HEAD = 64
RW_HEADS = D_MODEL // RW_HEAD
RW_DECAY_LORA = 64
RW_A_LORA = 64
RW_V_LORA = 32
RW_GATE_LORA = 160
ALPHA = (2.0 * DEPTH) ** 0.25
BETA = (8.0 * DEPTH) ** -0.25
LN_EPS = 1e-5
RMS_EPS = 1e-6
GN_EPS = 64e-5
F_MIN = 1e-30
NEG_BIG = -1e30

kernel_name = 'hybrid_hgrn2_diffattn_rwkv7_step'

def layer_norm(x, g, b):
    xf = x.astype(jnp.float32)
    mu = jnp.mean(xf, axis=-1, keepdims=True)
    var = jnp.mean(jnp.square(xf - mu), axis=-1, keepdims=True)
    y = (xf - mu) * lax.rsqrt(var + LN_EPS) * g.astype(jnp.float32) + b.astype(jnp.float32)
    return y.astype(x.dtype)

def rms_norm(x, g):
    xf = x.astype(jnp.float32)
    return xf * lax.rsqrt(jnp.mean(xf * xf, axis=-1, keepdims=True) + RMS_EPS) * g.astype(jnp.float32)

def head_group_norm(y, g, b):
    mu = jnp.mean(y, axis=-1, keepdims=True)
    var = jnp.mean(jnp.square(y - mu), axis=-1, keepdims=True)
    gh = g.reshape(RW_HEADS, RW_HEAD).astype(jnp.float32)
    bh = b.reshape(RW_HEADS, RW_HEAD).astype(jnp.float32)
    return (y - mu) * lax.rsqrt(var + GN_EPS) * gh + bh

def gather_pages(pool, page_table):
    g = pool[page_table]
    return g.reshape((g.shape[0], g.shape[1] * g.shape[2]) + g.shape[3:])

def hgrn2_chunkwise(q, k, v, log_f, s0):
    B, L, H, DK = q.shape
    C = math.gcd(L, HG_CHUNK)
    nc = L // C

    def to_chunks(t):
        return t.reshape(B, nc, C, H, t.shape[-1]).transpose(1, 0, 2, 3, 4)

    causal = jnp.tril(jnp.ones((C, C), dtype=bool))[None, :, :, None, None]

    def step(S, inp):
        qc, kc, vc, gc = inp
        b = jnp.cumsum(gc, axis=1)
        inter = jnp.einsum('bthd,bhdv->bthv', qc * jnp.exp(b), S)
        rel = b[:, :, None] - b[:, None, :]
        decay = jnp.where(causal, jnp.exp(jnp.where(causal, rel, 0.0)), 0.0)
        scores = jnp.einsum('bthd,btshd,bshd->bhts', qc, decay, kc)
        intra = jnp.einsum('bhts,bshv->bthv', scores, vc)
        b_last = b[:, -1]
        S = jnp.exp(b_last)[..., None] * S + jnp.einsum(
            'bshd,bshv->bhdv', kc * jnp.exp(b_last[:, None] - b), vc)
        return S, inter + intra

    s_fin, o = lax.scan(step, s0, (to_chunks(q), to_chunks(k), to_chunks(v), to_chunks(log_f)))
    o = o.transpose(1, 0, 2, 3, 4).reshape(B, L, H, v.shape[-1])
    return o, s_fin

def hgrn2_mix(hq, hf, hi, hg, lb, norm_g, s0):
    B, L, _ = hq.shape

    def heads(t):
        return t.reshape(B, L, HG_HEADS, HG_DK).astype(jnp.float32)

    q = jax.nn.silu(heads(hq))
    lbh = lb.reshape(HG_HEADS, HG_DK)
    f = lbh + (1.0 - lbh) * jax.nn.sigmoid(heads(hf))
    log_f = jnp.log(jnp.maximum(f, F_MIN))
    k = 1.0 - f
    o, s = hgrn2_chunkwise(q, k, heads(hi), log_f, s0.astype(jnp.float32))
    o = rms_norm(o, norm_g) * jax.nn.sigmoid(heads(hg))
    return o.reshape(B, L, HG_WIDTH).astype(hq.dtype), s.astype(s0.dtype)

def diff_attn_block(q, k, v, q_start, lam):
    T = q.shape[1]
    L = k.shape[1]
    s = jnp.einsum('bthcd,blhcd->bhctl', q, k).astype(jnp.float32) * (DA_DH ** -0.5)
    allowed = jnp.arange(L)[None, :] <= (q_start + jnp.arange(T))[:, None]
    s = jnp.where(allowed, s, NEG_BIG)
    p = jax.nn.softmax(s, axis=-1)
    w = p[:, :, 0] - lam * p[:, :, 1]
    return jnp.einsum('bhtl,blhv->bthv', w.astype(v.dtype), v)

def diff_attn_prompt(q, k, v, lam):
    B, S = q.shape[0], q.shape[1]
    qb = math.gcd(S, Q_BLOCK)
    nb = S // qb
    q_blocks = q.reshape(B, nb, qb, DA_HEADS, 2, DA_DH).swapaxes(0, 1)
    starts = jnp.arange(nb) * qb
    out = lax.map(lambda a: diff_attn_block(a[0], k, v, a[1], lam), (q_blocks, starts))
    return out.swapaxes(0, 1).reshape(B, S, DA_HEADS, DA_DV)

def even_mixer(x, hg_s0, past_k, past_v, lb, lam, lam_init, W, j):
    B, L, _ = x.shape
    proj = x @ W['w_in_even'][j]
    hq, hf, hi, hg, dq, dk, dv = jnp.split(proj, IN_SPLITS, axis=-1)
    o_h, s_hg = hgrn2_mix(hq, hf, hi, hg, lb, W['hg_norm_g'][j], hg_s0)
    q = dq.reshape(B, L, DA_HEADS, 2, DA_DH)
    k = dk.reshape(B, L, DA_HEADS, 2, DA_DH)
    v = dv.reshape(B, L, DA_HEADS, DA_DV)
    if past_k is None:
        o_d = diff_attn_prompt(q, k, v, lam)
    else:
        k_all = jnp.concatenate([past_k.astype(k.dtype), k], axis=1)
        v_all = jnp.concatenate([past_v.astype(v.dtype), v], axis=1)
        o_d = diff_attn_block(q, k_all, v_all, past_k.shape[1], lam)
    o_d = (rms_norm(o_d, W['da_norm_g'][j]) * (1.0 - lam_init)).reshape(B, L, DA_WIDTH).astype(x.dtype)
    out = jnp.concatenate([o_h, o_d], axis=-1) @ W['w_out_even'][j]
    return out, s_hg, k, v

def rwkv7_scan(r, w, k, v, a, b, s0):
    def step(S, inp):
        rt, wt, kt, vt, at, bt = inp
        sa = jnp.einsum('bhij,bhj->bhi', S, at)
        S = S * wt[:, :, None, :] + sa[..., None] * bt[:, :, None, :] + vt[..., None] * kt[:, :, None, :]
        return S, jnp.einsum('bhij,bhj->bhi', S, rt)

    seq = tuple(t.swapaxes(0, 1) for t in (r, w, k, v, a, b))
    S, y = lax.scan(step, s0, seq)
    return y.swapaxes(0, 1), S

def rwkv7_mixer(x, shift0, wkv0, v_first, W, j):
    B, L, D = x.shape
    x_prev = jnp.concatenate([shift0[:, None, :].astype(x.dtype), x[:, :-1]], axis=1)
    xx = x_prev - x
    mix = W['rw_mix'][j]
    xr, xw, xk, xv, xa, xg = (x + xx * mix[m] for m in range(6))
    r = xr @ W['rw_w_r'][j]
    k = xk @ W['rw_w_k'][j]
    v = xv @ W['rw_w_v'][j]
    w = -jax.nn.softplus(-(W['rw_w0'][j] + jnp.tanh(xw @ W['rw_w1'][j]) @ W['rw_w2'][j])) - 0.5
    if j == 0:
        v_first = v
    else:
        v = v + (v_first - v) * jax.nn.sigmoid(
            W['rw_v0'][j - 1] + (xv @ W['rw_v1'][j - 1]) @ W['rw_v2'][j - 1])
    a = jax.nn.sigmoid(W['rw_a0'][j] + (xa @ W['rw_a1'][j]) @ W['rw_a2'][j])
    g = jax.nn.sigmoid(xg @ W['rw_g1'][j]) @ W['rw_g2'][j]

    def heads(t):
        return t.reshape(B, L, RW_HEADS, RW_HEAD).astype(jnp.float32)

    kk = heads(k * W['rw_k_k'][j])
    kk = kk / jnp.maximum(jnp.sqrt(jnp.sum(kk * kk, axis=-1, keepdims=True)), 1e-12)
    k = k * (1.0 + (a - 1.0) * W['rw_k_a'][j])
    rh, kh, vh, ah = heads(r), heads(k), heads(v), heads(a)
    decay = jnp.exp(-jnp.exp(heads(w)))
    y, s = rwkv7_scan(rh, decay, kh, vh, -kk, kk * ah, wkv0.astype(jnp.float32))
    y = head_group_norm(y, W['rw_lnx_g'][j], W['rw_lnx_b'][j])
    y = y + jnp.sum(rh * kh * W['rw_r_k'][j].astype(jnp.float32), axis=-1, keepdims=True) * vh
    out = (y.reshape(B, L, D).astype(x.dtype) * g) @ W['rw_w_o'][j]
    return out, x[:, -1], s.astype(wkv0.dtype), v_first

def trunk(x, p, hg_s0, wkv_s0, shift0, cache_k, cache_v, page_table, W):
    lb_sm = jax.nn.softmax(W['hg_lb_logits'].astype(jnp.float32), axis=0)
    lower_bounds = jnp.cumsum(lb_sm, axis=0) - lb_sm[0]
    new_k, new_v, new_hg, new_wkv, new_shift = [], [], [], [], []
    v_first = None
    for i in range(DEPTH):
        j = i // 2
        if i % 2 == 0:
            if page_table is None:
                past_k = None
                past_v = None
            else:
                past_k = gather_pages(cache_k[j], page_table)
                past_v = gather_pages(cache_v[j], page_table)
            lam_init = 0.8 - 0.6 * math.exp(-0.3 * i)
            lam = (jnp.exp(jnp.sum(W['da_lam_q1'][j] * W['da_lam_k1'][j]).astype(jnp.float32))
                   - jnp.exp(jnp.sum(W['da_lam_q2'][j] * W['da_lam_k2'][j]).astype(jnp.float32))
                   + lam_init)
            h, s_hg, k_rows, v_rows = even_mixer(x, hg_s0[j], past_k, past_v, lower_bounds[j],
                                                 lam, lam_init, W, j)
            new_k.append(k_rows)
            new_v.append(v_rows)
            new_hg.append(s_hg)
        else:
            h, sh, s_wkv, v_first = rwkv7_mixer(x, shift0[j], wkv_s0[j], v_first, W, j)
            new_shift.append(sh)
            new_wkv.append(s_wkv)
        x = layer_norm(ALPHA * x + h, W['ln1_g'][i], W['ln1_b'][i])
        hid = jax.nn.relu(x @ W['mlp_up'][i])
        x = layer_norm(ALPHA * x + (hid * hid) @ W['mlp_down'][i], W['ln2_g'][i], W['ln2_b'][i])
        x = x + jax.nn.sigmoid(x @ W['ple_gate'][i]) * (p[i] @ W['ple_proj'][i])
    return (x, jnp.stack(new_k), jnp.stack(new_v), jnp.stack(new_hg),
            jnp.stack(new_wkv), jnp.stack(new_shift))

def setup_inputs(seed: int = 0) -> dict:
    key = jax.random.key(seed)
    ks = iter(jax.random.split(key, 64))

    def nrm(shape, scale=1.0):
        return jax.random.normal(next(ks), shape, jnp.float32) * scale

    def unif(shape, lo, hi):
        return jax.random.uniform(next(ks), shape, jnp.float32, lo, hi)

    def gain(shape):
        return 1.0 + nrm(shape, 0.02)

    n_pages = PAST_LEN // PAGE_SIZE
    n_used = DEC_BATCH * n_pages
    n_phys = n_used + max(1, n_used // 4)
    page_table = jax.random.permutation(next(ks), n_phys)[:n_used].reshape(DEC_BATCH, n_pages).astype(jnp.int32)
    d = D_MODEL
    rd = d ** -0.5
    return {
        'x_prompt': nrm((BATCH, SEQ, d)),
        'x_sample': nrm((DEC_BATCH, DEC_SEQ, d)),
        'cache_k': nrm((N_EVEN, n_phys, PAGE_SIZE, DA_HEADS, 2, DA_DH)),
        'cache_v': nrm((N_EVEN, n_phys, PAGE_SIZE, DA_HEADS, DA_DV)),
        'state_hgrn': nrm((N_EVEN, DEC_BATCH, HG_HEADS, HG_DK, HG_DV)),
        'state_wkv': nrm((N_ODD, DEC_BATCH, RW_HEADS, RW_HEAD, RW_HEAD), 0.5),
        'state_shift': nrm((N_ODD, DEC_BATCH, d)),
        'page_table': page_table,
        'p_prompt': nrm((DEPTH, BATCH, SEQ, PLE_DIM)),
        'p_sample': nrm((DEPTH, DEC_BATCH, DEC_SEQ, PLE_DIM)),
        'w_in_even': nrm((N_EVEN, d, IN_COLS), rd),
        'w_out_even': nrm((N_EVEN, d, d), rd * BETA),
        'hg_lb_logits': nrm((N_EVEN, HG_WIDTH), 0.5),
        'hg_norm_g': gain((N_EVEN, HG_DV)),
        'da_lam_q1': nrm((N_EVEN, DA_DH), 0.1),
        'da_lam_k1': nrm((N_EVEN, DA_DH), 0.1),
        'da_lam_q2': nrm((N_EVEN, DA_DH), 0.1),
        'da_lam_k2': nrm((N_EVEN, DA_DH), 0.1),
        'da_norm_g': gain((N_EVEN, DA_DV)),
        'rw_mix': unif((N_ODD, 6, d), 0.0, 1.0),
        'rw_w_r': nrm((N_ODD, d, d), rd),
        'rw_w_k': nrm((N_ODD, d, d), rd),
        'rw_w_v': nrm((N_ODD, d, d), rd),
        'rw_w_o': nrm((N_ODD, d, d), rd * BETA),
        'rw_w0': unif((N_ODD, d), -6.5, -1.5),
        'rw_w1': nrm((N_ODD, d, RW_DECAY_LORA), rd),
        'rw_w2': nrm((N_ODD, RW_DECAY_LORA, d), 0.5 * RW_DECAY_LORA ** -0.5),
        'rw_a0': nrm((N_ODD, d), 0.1),
        'rw_a1': nrm((N_ODD, d, RW_A_LORA), rd),
        'rw_a2': nrm((N_ODD, RW_A_LORA, d), 0.5 * RW_A_LORA ** -0.5),
        'rw_v0': 1.0 + nrm((N_ODD - 1, d), 0.1),
        'rw_v1': nrm((N_ODD - 1, d, RW_V_LORA), rd),
        'rw_v2': nrm((N_ODD - 1, RW_V_LORA, d), 0.5 * RW_V_LORA ** -0.5),
        'rw_g1': nrm((N_ODD, d, RW_GATE_LORA), rd),
        'rw_g2': nrm((N_ODD, RW_GATE_LORA, d), RW_GATE_LORA ** -0.5),
        'rw_k_k': 0.85 + nrm((N_ODD, d), 0.02),
        'rw_k_a': gain((N_ODD, d)),
        'rw_r_k': nrm((N_ODD, RW_HEADS, RW_HEAD), 0.1),
        'rw_lnx_g': gain((N_ODD, d)),
        'rw_lnx_b': nrm((N_ODD, d), 0.02),
        'ln1_g': gain((DEPTH, d)),
        'ln1_b': nrm((DEPTH, d), 0.02),
        'ln2_g': gain((DEPTH, d)),
        'ln2_b': nrm((DEPTH, d), 0.02),
        'mlp_up': nrm((DEPTH, d, D_FF), rd),
        'mlp_down': nrm((DEPTH, D_FF, d), D_FF ** -0.5 * BETA),
        'ple_proj': nrm((DEPTH, PLE_DIM, d), PLE_DIM ** -0.5),
        'ple_gate': nrm((DEPTH, d, d), rd),
    }

def reference(x_prompt, x_sample, cache_k, cache_v, state_hgrn, state_wkv, state_shift, page_table,
              p_prompt, p_sample, w_in_even, w_out_even, hg_lb_logits, hg_norm_g,
              da_lam_q1, da_lam_k1, da_lam_q2, da_lam_k2, da_norm_g,
              rw_mix, rw_w_r, rw_w_k, rw_w_v, rw_w_o, rw_w0, rw_w1, rw_w2,
              rw_a0, rw_a1, rw_a2, rw_v0, rw_v1, rw_v2, rw_g1, rw_g2,
              rw_k_k, rw_k_a, rw_r_k, rw_lnx_g, rw_lnx_b,
              ln1_g, ln1_b, ln2_g, ln2_b, mlp_up, mlp_down, ple_proj, ple_gate):
    W = dict(w_in_even=w_in_even, w_out_even=w_out_even, hg_lb_logits=hg_lb_logits,
             hg_norm_g=hg_norm_g, da_lam_q1=da_lam_q1, da_lam_k1=da_lam_k1,
             da_lam_q2=da_lam_q2, da_lam_k2=da_lam_k2, da_norm_g=da_norm_g,
             rw_mix=rw_mix, rw_w_r=rw_w_r, rw_w_k=rw_w_k, rw_w_v=rw_w_v, rw_w_o=rw_w_o,
             rw_w0=rw_w0, rw_w1=rw_w1, rw_w2=rw_w2, rw_a0=rw_a0, rw_a1=rw_a1, rw_a2=rw_a2,
             rw_v0=rw_v0, rw_v1=rw_v1, rw_v2=rw_v2, rw_g1=rw_g1, rw_g2=rw_g2,
             rw_k_k=rw_k_k, rw_k_a=rw_k_a, rw_r_k=rw_r_k, rw_lnx_g=rw_lnx_g, rw_lnx_b=rw_lnx_b,
             ln1_g=ln1_g, ln1_b=ln1_b, ln2_g=ln2_g, ln2_b=ln2_b,
             mlp_up=mlp_up, mlp_down=mlp_down, ple_proj=ple_proj, ple_gate=ple_gate)
    B = x_prompt.shape[0]
    dt = x_prompt.dtype
    hg0 = jnp.zeros((N_EVEN, B, HG_HEADS, HG_DK, HG_DV), dt)
    wkv0 = jnp.zeros((N_ODD, B, RW_HEADS, RW_HEAD, RW_HEAD), dt)
    sh0 = jnp.zeros((N_ODD, B, D_MODEL), dt)
    y_prompt, k_prompt, v_prompt, hgrn_prompt, wkv_prompt, shift_prompt = trunk(
        x_prompt, p_prompt, hg0, wkv0, sh0, None, None, None, W)
    y_sample, k_sample, v_sample, hgrn_sample, wkv_sample, shift_sample = trunk(
        x_sample, p_sample, state_hgrn, state_wkv, state_shift, cache_k, cache_v, page_table, W)
    return (y_prompt, y_sample, k_prompt, v_prompt, k_sample, v_sample,
            hgrn_prompt, hgrn_sample, wkv_prompt, wkv_sample, shift_prompt, shift_sample)


_drawn_inputs = setup_inputs


def setup_inputs(seed=0):
    import zlib

    import numpy as np

    out = dict(_drawn_inputs(seed))
    spreads = {}
    factors = {'state_hgrn': 3.285,
     'hg_norm_g': 28.558,
     'da_lam_q1': 8.0,
     'da_norm_g': 23.003,
     'rw_lnx_g': 31.789,
     'rw_lnx_b': 28.788}
    for name, (base, spread) in spreads.items():
        noise = np.random.default_rng([zlib.crc32(name.encode()), seed]).standard_normal(out[name].shape)
        drawn = base * np.exp(spread * noise) if base else spread * noise
        out[name] = jnp.asarray(drawn.astype(out[name].dtype))
    for name, factor in factors.items():
        out[name] = (out[name] * factor).astype(out[name].dtype)
    return out
```

```python
import math
from contextlib import ExitStack

import concourse.bass as bass
from concourse import mybir

F32 = mybir.dt.float32
BF16 = mybir.dt.bfloat16
I32 = mybir.dt.int32
ALU = mybir.AluOpType
ACT = mybir.ActivationFunctionType
AX = mybir.AxisListType

P = 128
D = 1024
KT = D // P
TP = 1024
NSEQ, LSEQ = 8, 8
TS = NSEQ * LSEQ
T = TP + TS
BLKS = TP // P
HEADS = 4
FF = 4 * D
PLE = 256
PAGES = 8
PAGE = 128
ALPHA = 4.0 ** 0.25
LAM_INIT = 0.8 - 0.6
SPANS = [(0, 512), (512, 512), (1024, TS)]
QUAD = T // 4
SLOTS = 6
BANK = 512
NEG = -1e30
LEVELS = 7
CH = 64
NCH = TP // CH
RWL = 6

STAGES = {
    "in": (4, 7, 7), "out": (2, 4, 4),
    "up0": (8, 4, 4), "down0": (4, 2, 8), "ple0": (4, 4, 4),
    "lora": (1, 4, 4), "r": (2, 4, 4), "k": (2, 4, 4), "v": (2, 4, 4),
    "rout": (2, 4, 4),
    "up1": (8, 4, 4), "down1": (4, 2, 8), "ple1": (4, 4, 4),
}


def before(stage, count):
    total = 0
    for name, sizes in STAGES.items():
        if name == stage:
            return total
        total += count(*sizes)


def unit(stage, i, u):
    _, _, per = STAGES[stage]
    slot = u % SLOTS
    in_trip = len(range(slot, per, SLOTS))
    base = before(stage, lambda t, j, n: t * len(range(slot, n, SLOTS)))
    return slot, i * in_trip + (base + u // SLOTS)


def job(stage, i, j):
    _, per, _ = STAGES[stage]
    q = j % 2
    in_trip = len(range(q, per, 2))
    base = before(stage, lambda t, n, u: t * len(range(q, n, 2)))
    return q, i * in_trip + (base + j // 2), i * per + (before(stage, lambda t, n, u: t * n) + j)


def trunk_program(nc, a, o):
    with ExitStack() as ctx:
        def sb(name, cols, dt=F32, rows=P):
            return ctx.enter_context(nc.sbuf_tensor(name, [rows, cols], dt))

        def sem(name):
            return ctx.enter_context(nc.semaphore(name))

        xa = sb("xa", KT * T)
        big = sb("big", FF // P * T)
        ring = sb("ring", SLOTS * 1024)
        ident = sb("ident", P)
        ones = sb("ones", P)
        headones = sb("headones", P)
        ist = sb("ist", 64)
        par = sb("par", 256)
        causal = sb("causal", P)
        newmask = sb("newmask", 64)
        cst = sb("cst", 16)
        cur = sb("cur", 16)
        small = sb("small", 64)
        qa = sb("qa", P)
        reset = sb("reset", T, BF16)
        state = sb("state", 2 * P)
        accum = sb("accum", 1152)
        lora2 = sb("lora2", 3 * P)
        pages = ctx.enter_context(nc.sbuf_tensor("pages", [1, NSEQ * PAGES], I32))
        ps = ctx.enter_context(nc.psum_tensor("ps", [P, 8 * BANK], F32))

        EPS_LN, EPS_RMS, EPS_GN, TEN_LN2, NLAM, LAMC = (cst[:, n:n + 1] for n in range(6))

        def xs(t, k, lo=0, n=T):
            return t[:, k * T + lo:k * T + lo + n]

        def blocks(t, width=P):
            return t[:, 0:BLKS * width].rearrange("p (n c) -> p n c", c=width)

        def carve(start, sizes, of=None):
            of = big if of is None else of
            got, at = {}, start
            for name, cols in sizes:
                got[name] = of[:, at:at + cols]
                at += cols
            return got

        e = carve(KT * T, [("QH", T), ("GH", T), ("HG", T), ("T1", T),
                           ("FH", T), ("QB", T), ("EB", T), ("ML", LEVELS * T),
                           ("VH", 1152), ("SC", T), ("GM", 1024), ("S0", 1024),
                           ("DQ", T), ("DK", T), ("DV", 1152), ("RM", T), ("MK", 1024), ("KO", 1152)])
        e.update(carve((KT + 7) * T, [("SS", 1152), ("KDT", 1152), ("VM", 1024), ("SN", 1024)]))
        e.update(carve((KT + 4) * T, [("P0", T), ("P1", T), ("WT", 1024), ("QP", T), ("KV", 3 * 1024),
                                      ("KTS", 1024), ("WTS", 576)]))
        lo8 = big[:, 0:KT * T]
        mixed = [big[:, KT * T:2 * KT * T], big[:, 2 * KT * T:3 * KT * T]]
        xin = big[:, 0:9 * D]
        prow = e["SC"][:, 0:256]
        lamv = e["GM"][:, 0:256]
        pl = carve(8 * T, [("ROWS", 9 * PLE), ("PT", 2 * T), ("GATE", 2 * T), ("TMP", T)])
        ln = carve(24 * T, [("VACC", T), ("SQ0", T), ("SQ1", T), ("RSTD", T)])
        yout = big[:, KT * T:KT * T + 9 * D]
        hid_wa, hid_g1, hid_g2, rwm = (big[:, (24 + n) * T:(25 + n) * T] for n in range(4))
        gmask = rwm[:, 0:256]
        smask = rwm[0:64, 256:384]
        lmask = rwm[:, 384:384 + RWL * CH]
        bmask = cst[0:64, 8:16]
        rows4 = [big[:, (28 + n) * T:(29 + n) * T] for n in range(4)]
        w = carve(8 * T, [("R", T), ("K", T), ("V", T), ("GT", T), ("BON", T), ("AR", 2 * T), ("BK", 2 * T),
                          ("LW", T), ("C", T), ("EPP", T), ("EP", T), ("KK", T), ("RN", T), ("SA", T)])
        w.update(carve(28 * T, [("KTK", 1152), ("VTK", 1152), ("WS", 1024), ("ST0", 1024)]))
        w.update(carve(8 * T, [("AB", 2 * T)]))
        w.update(carve(17 * T, [("X", T), ("P1M", T), ("XT0", T), ("XT1", T), ("TAT", T), ("AKV", 1152)]))
        w.update(carve(17 * T, [("US", 1152)]))
        w.update(carve(0, [("RB0", 2 * T), ("RB1", 2 * T), ("ATK", 1152)], ring))
        w["BTK"] = accum
        w["TATM"], w["USM"], w["VM"] = w["AR"][:, 0:576], w["BK"][:, 0:1024], w["BK"][:, T:T + 1024]
        w["YS"], w["SQ"], w["RS"], w["SO"] = w["XT0"], w["XT1"], w["TAT"], w["ATK"]

        w_land = [sem(f"w_land{s}") for s in range(SLOTS)]
        w_used = [sem(f"w_used{s}") for s in range(SLOTS)]
        job_done = sem("job_done")
        job_free = [sem(f"job_free{q}") for q in range(2)]
        (in_rows, in_x, in_misc, consts, par_tr, par_ok, xt_done, xt_copied, lam_ok,
         in_evac, hg_pre, hg_exp, hg_ready, gram_done, gram_used, kdt_done, kdt_ok, vm_ok, u_done, us_done,
         states_ok, sn_ok, s0_land, o_done, o_sq, ss_done, rinv_ok, hg_done, hg_stored,
         ko_done, ko_ok, kv_stored, qp_ok, qk_done, nmax_ok, probs_ok, w_ok, wtr_done, wt_ok, pv_done,
         ktr_done, kta_ok, ktd_ok, sqk_done, s_nmax, s_probs, s_comb, swt_done, swt_ok, so_done, so_sq, sss_done,
         srinv, attn_done, kv_used) = (sem(n) for n in (
            "in_rows in_x in_misc consts par_tr par_ok xt_done xt_copied lam_ok "
            "in_evac hg_pre hg_exp hg_ready gram_done gram_used kdt_done kdt_ok vm_ok u_done us_done "
            "states_ok sn_ok s0_land o_done o_sq ss_done rinv_ok hg_done hg_stored "
            "ko_done ko_ok kv_stored qp_ok qk_done nmax_ok probs_ok w_ok wtr_done wt_ok pv_done "
            "ktr_done kta_ok ktd_ok sqk_done s_nmax s_probs s_comb swt_done swt_ok so_done so_sq sss_done "
            "srinv attn_done kv_used").split())
        passed = sem("passed")
        kv_land = [sem(f"kv_land{n}") for n in range(3)]
        kv_odd_land = [sem(f"kv_odd_land{n}") for n in range(3)]
        (ln_acc, ln_mean, ln_xc, ln_sq, ln_sqsum, ln_var, ln_rstd, ln_y, ln_done, relu_ok, hid_ok,
         p_land, pt_tr, pt_ok, gate_ok, ple_ct) = (sem(n) for n in (
            "ln_acc ln_mean ln_xc ln_sq ln_sqsum ln_var ln_rstd ln_y ln_done relu_ok hid_ok "
            "p_land pt_tr pt_ok gate_ok ple_ct").split())
        rkv_st = [sem(f"rkv_st{n}") for n in range(4)]
        (sg_ok, sg_tr, sg_rows, shift_stored, xm_ok, xm_used, lora_ok, rw_masks, rkv_land, lora2_land, ws_land,
         rw_mm, rw_dve, rw_act, rw_tr, rw_trc, gr_done, gr_used, p1_done, p1m_ok, x_done, x_ok, akv_done, akv_ok,
         tat_done, tat_ok, rkv_used, ws_tr, ws_ok, us_mm, us_cp, st_mm, st_ok, tatm_ok, usm_ok, y_done, y_ok,
         sst_mm, sst_ok, so_tr, so_ok, wkv_stored, gn_mm, gn_dve, gn_act, rw_out, y_tr, y_rows, y_stored) = (
            sem(n) for n in (
            "sg_ok sg_tr sg_rows shift_stored xm_ok xm_used lora_ok rw_masks rkv_land lora2_land ws_land "
            "rw_mm rw_dve rw_act rw_tr rw_trc gr_done gr_used p1_done p1m_ok x_done x_ok akv_done akv_ok "
            "tat_done tat_ok rkv_used ws_tr ws_ok us_mm us_cp st_mm st_ok tatm_ok usm_ok y_done y_ok "
            "sst_mm sst_ok sot_tr sot_ok wkv_stored gn_mm gn_dve gn_act rw_out y_tr y_rows y_stored").split())

        scratch = nc.dram_tensor("rkv_scratch", [3, KT, P, T], F32, kind="Internal").ap()

        def pset(q, lo=0, n=T, r0=0, r1=P):
            return ps[r0:r1, q * 3 * BANK + lo:q * 3 * BANK + lo + n]

        def quad(q, r0=0, r1=P):
            return ps[r0:r1, q * 4 * BANK:(q + 1) * 4 * BANK].rearrange("p (b c) -> p b c", c=BANK)[:, :, 0:QUAD]

        def quads(t):
            return t.rearrange("p (b c) -> p b c", c=QUAD)

        def bank(b, n=BANK, lo=0, r0=0, r1=P):
            return ps[r0:r1, b * BANK + lo:b * BANK + lo + n]

        def load_pages(eng, i, odd, land):
            eng.wait_ge(hg_done, i + 1)
            eng.wait_ge(hg_stored, 32 * i + 32)
            eng.sem_inc(passed, 1)
            for n in range(2 * NSEQ):
                cache = a["cache_k"][0].rearrange("n p h c d -> n p h (c d)") if n < NSEQ else a["cache_v"][0]
                if n >= 3:
                    eng.wait_ge(kv_used, i * 16 + n - 2)
                    eng.sem_inc(passed, 1)
                for g in range(odd, PAGES, 2):
                    page = eng.value_load(pages[0:1, n % NSEQ * PAGES + g:n % NSEQ * PAGES + g + 1],
                                          min_val=0, max_val=a["cache_k"].shape[1] - 1)
                    eng.dma_start(e["KV"][:, (n % 3) * 1024 + g * P:(n % 3) * 1024 + (g + 1) * P],
                                  cache[bass.ds(page, 1), :, bass.ds(i, 1), :].rearrange("a p b d -> p (a b d)")
                                  ).then_inc(land[n % 3], 16)

        block = ctx.enter_context(nc.Block())

        @block.sync
        def _(sp):
            rows0 = [(a[n], 16) for n in ("ln1_g", "ln1_b", "ln2_g", "ln2_b")] + [(a["rw_mix"], 48)]
            rows1 = [(a["state_shift"], 64)] + [(a[n], 8) for n in (
                "rw_w0", "rw_a0", "rw_k_k", "rw_k_a", "rw_lnx_g", "rw_lnx_b", "rw_r_k")] + [
                (a["hg_norm_g"], 1), (a["da_norm_g"], 1), (a["hg_lb_logits"], 4)]
            for half, rows in ((0, rows0), (1, rows1)):
                at = 0
                for src, n in rows:
                    flat = src.flatten().rearrange("(r c) -> r c", c=P)
                    sp.dma_start(prow[at:at + n, half * P:(half + 1) * P], flat).then_inc(in_rows, 16)
                    at += n
            sp.dma_start(pages[0:1, :], a["page_table"].flatten().rearrange("(a n) -> a n", a=1)).then_inc(in_misc, 16)
            for n, name in enumerate(("da_lam_q1", "da_lam_k1", "da_lam_q2", "da_lam_k2")):
                sp.dma_start(lamv[:, n * 64:(n + 1) * 64], a[name].broadcast_to([P, 64])).then_inc(in_misc, 16)
            sp.dma_start(xin[:, 0:BLKS * D].rearrange("p (n c) -> p n c", c=D),
                         a["x_prompt"][0].rearrange("(n p) c -> p n c", p=P)).then_inc(in_x, 16)
            sp.dma_start(xin[0:TS, BLKS * D:9 * D], a["x_sample"].rearrange("b t c -> (b t) c")).then_inc(in_x, 16)

            def load_unit(stage, i, u, src, kt=KT, width=P):
                slot, used = unit(stage, i, u)
                sp.wait_ge(w_used[slot], used + 1)
                dst = ring[:, slot * 1024:slot * 1024 + kt * width].rearrange("p (k c) -> p k c", c=width)
                sp.dma_start(dst, src.rearrange("(k p) c -> p k c", p=P)).then_inc(w_land[slot], 16)

            def load_in(i, jobs):
                for j in jobs:
                    part = (0, 1, 3, 2, 4, 5, 6)[j]
                    load_unit("in", i, j, a["w_in_even"][0][:, bass.ds(i * P + part * 512, P)])

            def load_s0(i):
                if not isinstance(i, int) or i:
                    sp.wait_ge(attn_done, i)
                sp.dma_start(e["S0"].rearrange("p (b v) -> p b v", v=P),
                             a["state_hgrn"][0][:, bass.ds(i, 1)].rearrange("b a k v -> k (a b) v")
                             ).then_inc(s0_land, 16)

            def load_kv(i):
                load_pages(sp, i, 0, kv_land)

            sp.wait_ge(in_misc, 5 * 16)
            load_in(0, range(7))
            load_s0(0)
            with sp.Fori(0, HEADS - 1) as i:
                load_in(i + 1, range(SLOTS))
                load_kv(i)
                load_s0(i + 1)
                load_in(i + 1, range(SLOTS, 7))
            load_kv(HEADS - 1)

            def load_square(stage, src):
                with sp.Fori(0, STAGES[stage][0]) as i:
                    for j in range(4):
                        load_unit(stage, i, j, src[:, bass.ds(i * 512 + j * P, P)])

            def load_mlp(layer):
                with sp.Fori(0, 8) as i:
                    for j in range(4):
                        load_unit(f"up{layer}", i, j, a["mlp_up"][layer][:, bass.ds(i * 512 + j * P, P)])
                with sp.Fori(0, 4) as i:
                    for j in range(2):
                        for g in range(4):
                            load_unit(f"down{layer}", i, j * 4 + g,
                                      a["mlp_down"][layer][g * 1024:(g + 1) * 1024, bass.ds(i * 256 + j * P, P)])
                sp.wait_ge(ln_acc, 2 * layer + 2)
                sp.dma_start(pl["ROWS"][:, 0:BLKS * PLE].rearrange("p (n c) -> p n c", c=PLE),
                             a["p_prompt"][layer, 0].rearrange("(n p) c -> p n c", p=P)).then_inc(p_land, 16)
                sp.dma_start(pl["ROWS"][0:TS, BLKS * PLE:9 * PLE],
                             a["p_sample"][layer].rearrange("b t c -> (b t) c")).then_inc(p_land, 16)
                with sp.Fori(0, 4) as i:
                    for j in range(2):
                        cols = bass.ds(i * 256 + j * P, P)
                        load_unit(f"ple{layer}", i, 2 * j, a["ple_gate"][layer][:, cols])
                        load_unit(f"ple{layer}", i, 2 * j + 1, a["ple_proj"][layer][:, cols], kt=2)

            load_square("out", a["w_out_even"][0])
            load_mlp(0)
            load_unit("lora", 0, 0, a["rw_w1"][0], width=64)
            load_unit("lora", 0, 1, a["rw_a1"][0], width=64)
            load_unit("lora", 0, 2, a["rw_g1"][0][:, 0:P])
            load_unit("lora", 0, 3, a["rw_g1"][0][:, P:160], width=32)
            for name in "rkv":
                load_square(name, a["rw_w_" + name][0])

            def load_core(i, first=False):
                cols = bass.ds(i * P, P)
                for n, name in enumerate("RKV"):
                    sp.dma_start(w[name], scratch[n, bass.ds(i, 1)].rearrange("a p t -> p (a t)")).then_inc(rkv_land, 16)
                sp.dma_start(lora2[0:64, 0:P], a["rw_w2"][0][:, cols]).then_inc(lora2_land, 16)
                sp.dma_start(lora2[64:P, 0:P], a["rw_a2"][0][:, cols]).then_inc(lora2_land, 16)
                sp.dma_start(lora2[:, P:2 * P], a["rw_g2"][0][0:P, cols]).then_inc(lora2_land, 16)
                sp.dma_start(lora2[0:32, 2 * P:3 * P], a["rw_g2"][0][P:160, cols]).then_inc(lora2_land, 16)
                if not first:
                    sp.wait_ge(ws_tr, i)
                for h in range(2):
                    src = a["state_wkv"][0][:, bass.ds(i * 2 + h, 1)].rearrange("b a v k -> v (a b) k")
                    dst = w["WS"].rearrange("p (b c) -> p b c", c=P)[h * 64:(h + 1) * 64, :, h * 64:(h + 1) * 64]
                    sp.dma_start(dst, src).then_inc(ws_land, 16)

            for n in range(4):
                sp.wait_ge(rkv_st[n], 16 + 16 * 6)
            sp.wait_ge(xm_used, 6)
            sp.wait_ge(rw_masks, 1)
            load_core(0, True)
            with sp.Fori(1, KT) as i:
                sp.wait_ge(rkv_used, i)
                load_core(i)
            sp.wait_ge(rw_out, KT)
            load_square("rout", a["rw_w_o"][0])
            load_mlp(1)
            for b in range(9):
                n = P if b < BLKS else TS
                dst = o["y_prompt"][0][b * P:(b + 1) * P, :] if b < BLKS else \
                    o["y_sample"].rearrange("b t c -> (b t) c")
                sp.wait_ge(y_rows, b + 1)
                sp.dma_start(dst, yout[0:n, b * D:(b + 1) * D]).then_inc(y_stored, 16)
            sp.wait_ge(y_stored, 9 * 16)
            sp.wait_ge(shift_stored, 2 * 16)
            sp.wait_ge(kv_stored, HEADS * 4 * 16)
            sp.wait_ge(hg_stored, HEADS * 2 * 16)
            sp.wait_ge(wkv_stored, KT * 4 * 16)

        @block.gpsimd
        def _(pool):
            def fill(t, value):
                pool.drain()
                pool.memset(t, value)

            def keep(t, pattern, base, cm, fill=0.0):
                pool.drain()
                pool.affine_select(out=t, in_=t, compare_op=ALU.is_ge, fill=fill, base=base,
                                   pattern=pattern, channel_multiplier=cm)

            def eye(t, n=P):
                fill(t, 1.0)
                keep(t, [[-1, n]], 0, 1)
                keep(t, [[1, n]], 0, -1)

            eye(ident[:, :])
            fill(ones[:, :], 1.0)
            fill(headones[:, :], 0.0)
            pool.drain()
            fill(headones[0:64, 0:64], 1.0)
            fill(headones[64:P, 64:P], 1.0)
            eye(ist[0:64, :], 64)
            eye(ist[64:P, :], 64)
            fill(causal[:, :], 0.0)
            keep(causal[:, :], [[-1, P]], 0, 1, NEG)
            fill(newmask[:, :], 0.0)
            for r in (0, 64):
                nm = newmask[r:r + 64, :]
                keep(nm, [[-1, 64]], 0, 1, NEG)
                keep(nm, [[8, 8], [0, 8]], 7, -1, NEG)
            for col, v in ((EPS_LN, 1e-5), (EPS_RMS, 1e-6), (EPS_GN, 64e-5), (TEN_LN2, 10 * math.log(2.0))):
                fill(col, v)
            fill(bmask, 1.0)
            keep(bmask, [[-8, 8]], 0, 1)
            keep(bmask, [[8, 8]], 7, -1)
            fill(qa[:, :], 0.0)
            fill(reset[:, :], 1.0)
            fill(e["RM"], 1.0)
            pool.drain()
            fill(reset[:, 0:TP:CH], 0.0)
            fill(reset[:, TP:T:LSEQ], 0.0)
            fill(e["RM"][:, 0:TP:P], 0.0)
            fill(e["RM"][:, TP:T:LSEQ], 0.0)
            eye(e["MK"][:, 0:P])
            for lv in range(1, LEVELS + 1):
                m = 1 << (lv - 1)
                mk = e["MK"][:, lv * P:(lv + 1) * P]
                fill(mk, 0.0)
                pool.drain()
                up = mk.rearrange("p (n h m) -> p n h m", h=2, m=m)[:, :, 1, :]
                fill(up, 1.0)
                keep(up, [[-2 * m, P // (2 * m)], [0, m]], 0, 1)
                keep(up, [[2 * m, P // (2 * m)], [0, m]], m - 1, -1)
            pool.drain().then_inc(consts, 1)

            pool.wait_ge(in_misc, 5 * 16)
            with pool.Fori(0, HEADS) as i:
                pool.wait_ge(states_ok, i + 1)
                pool.wait_ge(sn_ok, i + 1)
                pool.dma_start(o["hgrn_prompt"][0, 0, bass.ds(i, 1)].rearrange("a k v -> k (a v)"),
                               e["SS"][:, 8 * P:9 * P]).then_inc(hg_stored, 16)
                pool.dma_start(o["hgrn_sample"][0][:, bass.ds(i, 1)].rearrange("b a k v -> k (a b) v"),
                               e["SN"].rearrange("p (b v) -> p b v", v=P)).then_inc(hg_stored, 16)
                pool.wait_ge(ko_ok, i + 1)
                for name, t in (("k", e["KO"]), ("v", e["DV"])):
                    dp = o[name + "_prompt"][0, 0].flatten().rearrange("(n p c) -> p n c", p=P, c=512)
                    ds_ = o[name + "_sample"][0].flatten().rearrange("(r c) -> r c", c=512)
                    pool.dma_start(dp[:, :, bass.ds(i * P, P)], blocks(t)).then_inc(kv_stored, 16)
                    pool.dma_start(ds_[:, bass.ds(i * P, P)], t[0:TS, 1024:1152]).then_inc(kv_stored, 16)
                load_pages(pool, i, 1, kv_odd_land)

            def norm_sums(n):
                for k in range(KT):
                    pool.wait_ge(ln_sq, 8 * n + k + 1)
                    sq = ln["SQ0"] if k % 2 == 0 else ln["SQ1"]
                    if k == 0:
                        pool.tensor_copy(ln["VACC"], sq).then_inc(ln_sqsum, 1)
                    else:
                        pool.drain()
                        pool.tensor_tensor(ln["VACC"], ln["VACC"], sq, ALU.add).then_inc(ln_sqsum, 1)

            norm_sums(0)
            norm_sums(1)
            pool.wait_ge(ple_ct, 2 + KT)
            g3 = gmask.rearrange("p (r t) -> p r t", r=2)
            fill(gmask, 1.0)
            keep(g3, [[1, 2], [1, P]], -1, -1)
            pool.drain()
            fill(g3[0:64, :, 64:P], 0.0)
            s4 = smask.rearrange("p (r b t) -> p r b t", r=2, b=8)
            fill(smask, 1.0)
            keep(smask.rearrange("p (r t) -> p r t", r=2), [[1, 2], [1, 64]], -1, -1)
            keep(s4, [[0, 2], [-8, 8], [0, 8]], 0, 1)
            keep(s4, [[0, 2], [8, 8], [0, 8]], 7, -1)
            fill(lmask, 0.0)
            for lv in range(RWL):
                m = 1 << lv
                pool.drain()
                for r in (0, 64):
                    v = lmask[r:r + 64, lv * CH:(lv + 1) * CH].rearrange("p (n h m) -> p n h m", h=2, m=m)[:, :, 0, :]
                    fill(v, 1.0)
                    keep(v, [[-2 * m, CH // (2 * m)], [0, m]], -m, 1)
                    keep(v, [[2 * m, CH // (2 * m)], [0, m]], 2 * m - 1, -1)
            for n in range(4):
                pool.wait_ge(rkv_st[n], 16 + 16 * 6)
            fill(w["WS"], 0.0)
            pool.drain().then_inc(rw_masks, 1)
            with pool.Fori(0, KT) as i:
                pool.wait_ge(so_ok, i + 1)
                so = w["SO"].rearrange("p (b c) -> p b c", c=P)
                for h in range(2):
                    rows, cols = slice(h * 64, h * 64 + 64), slice(h * 64, h * 64 + 64)
                    pool.dma_start(o["wkv_sample"][0][:, bass.ds(i * 2 + h, 1)].rearrange("b a v k -> v (a b) k"),
                                   so[rows, 0:8, cols]).then_inc(wkv_stored, 16)
                    pool.dma_start(o["wkv_prompt"][0, 0, bass.ds(i * 2 + h, 1)].rearrange("a v k -> v (a k)"),
                                   so[rows, 8, cols]).then_inc(wkv_stored, 16)
            norm_sums(2)
            norm_sums(3)

        @block.scalar
        def _(act):
            def f(out, in_, func, **kw):
                return act.activation(out, in_, func, **kw)

            for q in range(2):
                act.drain().then_inc(job_free[q], 1)
            for n in range(4):
                act.drain().then_inc(rkv_st[n], 16)
            act.wait_ge(par_tr, 1)
            f(par[:, 0:112], bank(6, 112), ACT.Copy)
            f(par[:, P:P + 126], bank(6, 126, P), ACT.Copy)
            act.drain().then_inc(par_ok, 1)
            for k in range(KT):
                act.wait_ge(xt_done, k + 1)
                f(xs(xa, k), pset(k % 2), ACT.Copy).then_inc(xt_copied, 1)

            def rsqrt_mean(dst, src, n, eps):
                f(dst, src, ACT.Ln, scale=1.0 / n, bias=eps)
                act.drain()
                return f(dst, dst, ACT.Exp, scale=-0.5)

            def by_block(dst, q):
                f(dst[:, 0:1024], pset(q, 0, 1024), ACT.Copy)
                return f(dst[0:TS, 1024:1152], pset(q, 1024, P, 0, TS), ACT.Copy)

            act.wait_ge(lam_ok, 1)
            f(small[:, 20:22], small[:, 18:20], ACT.Exp)
            f(small[:, 12:16], small[:, 8:12], ACT.Exp)
            act.drain().then_inc(lam_ok, 1)

            with act.Fori(0, HEADS) as i:
                def job_is_done(j):
                    q, used, n = job("in", i, j)
                    act.wait_ge(job_done, n + 1)
                    return q

                q = job_is_done(0)
                f(e["T1"], pset(q), ACT.Sigmoid).then_inc(in_evac, 1)
                q = job_is_done(1)
                f(e["FH"], pset(q), ACT.Sigmoid).then_inc(job_free[q], 1)
                act.drain().then_inc(in_evac, 1)
                q = job_is_done(2)
                f(e["HG"], pset(q), ACT.Sigmoid).then_inc(job_free[q], 1)
                act.drain().then_inc(in_evac, 1)
                act.wait_ge(hg_pre, i * 10 + 1)
                f(e["T1"], e["T1"], ACT.Ln)
                f(e["EB"], e["EB"], ACT.Ln)
                act.drain().then_inc(hg_exp, 1)
                q = job_is_done(3)
                by_block(e["VH"], q).then_inc(job_free[q], 1)
                act.drain().then_inc(in_evac, 1)
                act.wait_ge(hg_pre, i * 10 + 2)
                f(e["EB"], e["GH"], ACT.Exp).then_inc(hg_exp, 1)
                act.wait_ge(hg_pre, i * 10 + 3)
                f(e["T1"], e["T1"], ACT.Exp).then_inc(hg_exp, 1)
                for lv in range(LEVELS):
                    act.wait_ge(hg_pre, i * 10 + 4 + lv)
                    n = T if lv < 3 else TP
                    t = e["ML"][:, lv * T:lv * T + n]
                    f(t, t, ACT.Exp).then_inc(hg_exp, 1)
                q = job_is_done(4)
                f(e["DQ"], pset(q), ACT.Copy).then_inc(job_free[q], 1)
                act.drain().then_inc(in_evac, 1)
                q = job_is_done(5)
                f(e["DK"], pset(q), ACT.Copy).then_inc(job_free[q], 1)
                act.drain().then_inc(in_evac, 1)
                q = job_is_done(6)
                by_block(e["DV"], q).then_inc(job_free[q], 1)
                act.drain().then_inc(in_evac, 1)
                act.wait_ge(kdt_done, i + 1)
                by_block(e["KDT"], 1)
                act.drain().then_inc(kdt_ok, 1)
                act.wait_ge(o_done, i + 1)
                f(e["QH"], pset(0), ACT.Square).then_inc(o_sq, 1)
                act.wait_ge(ss_done, i + 1)
                rsqrt_mean(e["T1"], pset(1), P, EPS_RMS).then_inc(rinv_ok, 1)
                act.wait_ge(ko_done, i + 1)
                by_block(e["KO"], 1)
                act.drain().then_inc(ko_ok, 1)
                act.wait_ge(hg_done, i + 1)
                act.wait_ge(hg_stored, 32 * i + 32)
                for qb in range(BLKS):
                    n = (qb + 1) * P
                    act.wait_ge(nmax_ok, i * 8 + qb + 1)
                    if qb:
                        act.wait_ge(wtr_done, i * 12 + (qb if qb < 5 else 2 * qb - 4))
                    f(e["P0"][:, 0:n], bank(3, n), ACT.Exp, scale=0.125, bias=small[:, 26:27],
                      accum_out=small[:, 28:29])
                    f(e["P1"][:, 0:n], bank(6, n), ACT.Exp, scale=0.125, bias=small[:, 27:28],
                      accum_out=small[:, 29:30])
                    act.drain().then_inc(probs_ok, 1)
                    for g in range(1 if qb < 4 else 2):
                        m = min(4, qb + 1 - 4 * g) * P
                        act.wait_ge(wtr_done, i * 12 + (qb if qb < 5 else 2 * qb - 4) + g + 1)
                        if g == 0 and qb:
                            act.wait_ge(pv_done, i * 8 + qb)
                        f(e["WT"][:, g * 512:g * 512 + m], bank(5, m), ACT.Copy)
                        act.drain().then_inc(wt_ok, 1)
                for b in range(NSEQ):
                    act.wait_ge(ktr_done, i * 16 + 2 * b + 1)
                    if b:
                        act.wait_ge(sqk_done, i * 16 + 2 * b - 1)
                    f(e["KTS"][:, 0:512], bank(6), ACT.Copy).then_inc(kta_ok, 1)
                act.wait_ge(s_nmax, i + 1)
                f(e["P0"], pset(1), ACT.Exp, scale=0.125, bias=small[:, 31:32], accum_out=small[:, 32:33])
                act.drain().then_inc(s_probs, 1)
                act.wait_ge(swt_done, i + 1)
                f(e["WTS"][:, 0:512], bank(6), ACT.Copy)
                f(e["WTS"][0:TS, 512:576], bank(7, 64, 0, 0, TS), ACT.Copy)
                act.drain().then_inc(swt_ok, 1)
                act.wait_ge(so_done, i + 1)
                f(e["P1"], pset(0), ACT.Square).then_inc(so_sq, 1)
                act.wait_ge(sss_done, i + 1)
                rsqrt_mean(e["P0"], pset(1), P, EPS_RMS).then_inc(srinv, 1)
                act.wait_ge(kv_stored, 64 * i + 64)

            def norm(n, src, dst, g, b):
                for k in range(KT):
                    act.wait_ge(ln_xc, 8 * n + k + 1)
                    if k >= 2:
                        act.wait_ge(ln_sqsum, 8 * n + k - 1)
                    f(ln["SQ0"] if k % 2 == 0 else ln["SQ1"], xs(src, k), ACT.Square).then_inc(ln_sq, 1)
                act.wait_ge(ln_var, n + 1)
                rsqrt_mean(ln["RSTD"], pset(1), D, EPS_LN).then_inc(ln_rstd, 1)
                for k in range(KT):
                    act.wait_ge(ln_y, 8 * n + k + 1)
                    f(xs(dst, k), xs(src, k), ACT.Identity, scale=par[:, g + k:g + k + 1],
                      bias=par[:, b + k:b + k + 1]).then_inc(ln_done, 1)

            def mlp(layer):
                with act.Fori(0, 8) as i:
                    for j in range(4):
                        q, used, n = job(f"up{layer}", i, j)
                        act.wait_ge(job_done, n + 1)
                        f(quads(big[:, bass.ds(i * 4 * T + j * T, T)]), quad(q), ACT.Relu).then_inc(job_free[q], 1)
                        act.drain().then_inc(relu_ok, 1)
                norm(2 * layer + 1, xa, xa, 32 + 8 * layer, 48 + 8 * layer)
                for k in range(2):
                    act.wait_ge(pt_tr, 2 * layer + k + 1)
                    f(xs(pl["PT"], k), pset(k), ACT.Copy)
                act.drain().then_inc(pt_ok, 1)
                with act.Fori(0, 4) as i:
                    for j in range(2):
                        q, used, n = job(f"ple{layer}", i, 2 * j)
                        act.wait_ge(job_done, n + 1)
                        act.wait_ge(ple_ct, i * 2 + (8 * layer + j + 1))
                        f(quads(xs(pl["GATE"], j)), quad(q), ACT.Sigmoid).then_inc(job_free[q], 1)
                        act.drain().then_inc(gate_ok, 1)

            norm(0, xa, xa, 0, 16)
            mlp(0)
            act.wait_ge(sg_tr, 1)
            f(rows4[2][0:72, 0:P], bank(7, P, QUAD, 0, 72), ACT.Copy)
            act.drain().then_inc(sg_rows, 1)
            act.dma_start(o["shift_prompt"][0].rearrange("a (k c) -> (a k) c", c=P),
                          rows4[2][0:8, 0:P]).then_inc(shift_stored, 16)
            act.dma_start(o["shift_sample"][0].rearrange("b (k c) -> (b k) c", c=P),
                          rows4[2][8:72, 0:P]).then_inc(shift_stored, 16)
            for j, (dst, src, func) in enumerate((
                    (hid_wa[0:64, :], (0, 64), ACT.Tanh), (hid_wa[64:P, :], (64, P), ACT.Copy),
                    (hid_g1, (0, P), ACT.Sigmoid), (hid_g2[0:32, :], (0, 32), ACT.Sigmoid))):
                q, used, n = job("lora", 0, j)
                act.wait_ge(job_done, n + 1)
                f(quads(dst), quad(q, *src), func).then_inc(job_free[q], 1)
            act.drain().then_inc(lora_ok, 1)
            act.wait_ge(shift_stored, 32)
            for m, name in enumerate("rkv"):
                with act.Fori(0, 2) as i:
                    for j in range(4):
                        q, used, n = job(name, i, j)
                        act.wait_ge(job_done, n + 1)
                        act.wait_ge(rkv_st[j], 16 * i + 16 * (2 * m + 1))
                        f(quads(rows4[j]), quad(q), ACT.Copy).then_inc(job_free[q], 1)
                        act.drain()
                        act.dma_start(scratch[m, bass.ds(i * 4 + j, 1)].rearrange("a p t -> p (a t)"),
                                      rows4[j]).then_inc(rkv_st[j], 16)

            with act.Fori(0, KT) as i:
                act.wait_ge(rw_dve, i * 5 + 1)
                act.wait_ge(rw_mm, i * 5 + 1)
                f(w["LW"], pset(0), ACT.Sigmoid, bias=cur[:, 0:1]).then_inc(rw_act, 1)
                act.wait_ge(rw_mm, i * 5 + 2)
                f(w["SA"], pset(1), ACT.Sigmoid, bias=cur[:, 1:2]).then_inc(rw_act, 1)
                act.wait_ge(rw_mm, i * 5 + 3)
                f(w["GT"], pset(0), ACT.Copy).then_inc(rw_act, 1)
                act.wait_ge(rw_dve, i * 5 + 2)
                f(w["RN"], w["KK"], ACT.Square).then_inc(rw_act, 1)
                f(w["EP"], w["C"], ACT.Exp)
                f(w["EPP"], w["EPP"], ACT.Exp)
                act.drain()
                f(w["C"], w["C"], ACT.Exp, scale=-1.0)
                act.drain().then_inc(rw_act, 1)
                act.wait_ge(rw_dve, i * 5 + 3)
                f(w["RN"], w["RN"], ACT.Ln)
                act.drain()
                f(w["RN"], w["RN"], ACT.Exp, scale=-0.5, bias=TEN_LN2).then_inc(rw_act, 1)
                for n, name in enumerate(("ATK", "BTK", "KTK", "VTK")):
                    act.wait_ge(rw_tr, i * 4 + n + 1)
                    by_block(w[name], (n + 1) % 2)
                    act.drain().then_inc(rw_trc, 1)
                for h in range(2):
                    act.wait_ge(akv_done, i * 2 + h + 1)
                    f(w["AKV"][:, h * 576:h * 576 + 512], bank(0), ACT.Copy)
                    f(w["AKV"][0:TS, h * 576 + 512:h * 576 + 576], bank(1, 64, 0, 0, TS), ACT.Copy)
                    act.drain().then_inc(akv_ok, 1)
                act.wait_ge(tat_done, i + 1)
                f(w["TAT"], pset(1), ACT.Copy).then_inc(tat_ok, 1)
                act.wait_ge(ws_tr, i + 1)
                f(w["ST0"], bank(6, 1024), ACT.Copy).then_inc(ws_ok, 1)
                for c in range(NCH + 1):
                    r, blk = (c % 2 * 64, c // 2) if c < NCH else (0, BLKS)
                    act.wait_ge(us_mm, i * 17 + c + 1)
                    f(w["US"][r:r + 64, blk * P:(blk + 1) * P], bank(3 + c % 2, P, 0, r, r + 64),
                      ACT.Copy).then_inc(us_cp, 1)
                act.wait_ge(y_done, i + 1)
                f(w["YS"], pset(0), ACT.Copy).then_inc(y_ok, 1)
                act.wait_ge(so_tr, i + 1)
                f(w["SO"], pset(1, 0, 1152), ACT.Copy)
                act.drain().then_inc(so_ok, 1)
                act.wait_ge(gn_dve, i * 2 + 1)
                f(w["SQ"], w["YS"], ACT.Square).then_inc(gn_act, 1)
                act.wait_ge(gn_mm, i * 2 + 2)
                rsqrt_mean(w["RS"], pset(0), 64, EPS_GN).then_inc(gn_act, 1)
                act.wait_ge(wkv_stored, i * 64 + 64)
            norm(2, lo8, xa, 8, 24)
            mlp(1)
            for b in range(0, 9, 2):
                n = P if b < BLKS else TS
                act.wait_ge(y_tr, b + 1)
                f(yout[0:n, b * D:(b + 1) * D], bank(b % 4 * 2, D, 0, 0, n), ACT.Copy)
                act.drain().then_inc(y_rows, 1)
                if b < BLKS:
                    act.wait_ge(y_rows, b + 2)

        @block.vector
        def _(v):
            def tt(out, x, y, op):
                return v.tensor_tensor(out, x, y, op)

            for _ in range(2):
                v.drain().then_inc(ple_ct, 1)
            v.wait_ge(in_misc, 5 * 16)
            tt(lamv[:, 0:64], lamv[:, 0:64], lamv[:, 64:128], ALU.mult)
            tt(lamv[:, 128:192], lamv[:, 128:192], lamv[:, 192:256], ALU.mult)
            v.drain()
            v.tensor_reduce(small[:, 18:19], lamv[:, 0:64], AX.X, ALU.add)
            v.tensor_reduce(small[:, 19:20], lamv[:, 128:192], AX.X, ALU.add)
            v.wait_ge(par_ok, 1)
            lb = par[:, 250:254]
            v.tensor_copy(small[:, 12:16], lb)
            v.drain()
            tt(small[:, 8:12], lb, small[:, 12:16], ALU.subtract)
            v.drain().then_inc(lam_ok, 1)
            v.wait_ge(lam_ok, 2)
            tt(small[:, 22:23], small[:, 20:21], small[:, 21:22], ALU.subtract)
            v.reciprocal(small[:, 8:12], small[:, 12:16])
            v.drain()
            v.tensor_scalar(NLAM, small[:, 22:23], LAM_INIT, -1.0, ALU.add, ALU.mult)
            tt(small[:, 12:16], small[:, 12:16], small[:, 8:12], ALU.mult)
            v.wait_ge(consts, 1)
            v.memset(LAMC, 1.0)
            v.drain()
            tt(small[:, 0:4], small[:, 12:16], small[:, 12:16], ALU.subtract)
            v.tensor_copy(cst[64:P, 5:6], cst[64:P, 4:5])
            v.drain()
            v.tensor_scalar(small[:, 4:8], small[:, 0:4], -1.0, 1.0, ALU.mult, ALU.add)
            v.drain()

            seqs = lambda t: t[:, TP:T].rearrange("p (b s) -> p b s", s=LSEQ)
            with v.Fori(0, HEADS) as i:
                v.tensor_copy(cur[:, 0:1], small[:, bass.ds(i, 1)])
                v.tensor_copy(cur[:, 1:2], small[:, bass.ds(i + 4, 1)])
                v.wait_ge(in_evac, i * 7 + 1)
                q, _, _ = job("in", 0, 0)
                tt(e["QH"], e["T1"], pset(q), ALU.mult).then_inc(job_free[q], 1)
                v.drain()
                v.wait_ge(in_evac, i * 7 + 2)
                v.tensor_scalar(e["FH"], e["FH"], cur[:, 1:2], cur[:, 0:1], ALU.mult, ALU.add)
                v.drain()
                v.tensor_scalar(e["T1"], e["FH"], 2.0 ** -50, None, ALU.max)
                v.tensor_scalar(e["EB"], e["FH"], 1e-30, 2.0 ** 50, ALU.max, ALU.mult)
                v.drain()
                v.tensor_scalar(e["EB"], e["EB"], 1.0, None, ALU.min)
                v.tensor_scalar(e["FH"], e["FH"], -1.0, 1.0, ALU.mult, ALU.add)
                v.drain().then_inc(hg_pre, 1)
                v.wait_ge(hg_exp, i * 10 + 1)
                tt(e["QB"], e["T1"], e["EB"], ALU.add)
                v.drain()
                v.tensor_tensor_scan(e["GH"], e["RM"], e["QB"], 0.0, ALU.mult, ALU.add)
                v.drain().then_inc(hg_pre, 1)
                b8 = blocks(e["GH"])
                tt(blocks(e["T1"]), b8[:, :, P - 1:P].broadcast_to([P, BLKS, P]), b8, ALU.subtract)
                tt(seqs(e["T1"]), seqs(e["GH"])[:, :, 7:8].broadcast_to([P, NSEQ, LSEQ]), seqs(e["GH"]), ALU.subtract)
                v.drain().then_inc(hg_pre, 1)

                def halves(t, lv):
                    m, n = 1 << lv, (T if lv < 3 else TP)
                    r = t[:, 0:n].rearrange("p (n h m) -> p n h m", h=2, m=m)
                    return r[:, :, 0, :], r[:, :, 1, :], m, n // (2 * m)

                for lv in range(LEVELS):
                    lo, up, m, n = halves(e["GH"], lv)
                    mlo, mup, _, _ = halves(e["ML"][:, lv * T:(lv + 1) * T], lv)
                    mid = lo[:, :, m - 1:m].broadcast_to([P, n, m])
                    tt(mup, up, mid, ALU.subtract)
                    tt(mlo, mid, lo, ALU.subtract)
                    v.drain().then_inc(hg_pre, 1)
                v.wait_ge(hg_exp, i * 10 + 2)
                tt(e["QB"], e["QH"], e["EB"], ALU.mult)
                v.wait_ge(hg_exp, i * 10 + 3)
                tt(e["T1"], e["T1"], e["FH"], ALU.mult)
                for lv in range(LEVELS):
                    v.wait_ge(hg_exp, i * 10 + 4 + lv)
                    mlo, mup, _, _ = halves(e["ML"][:, lv * T:(lv + 1) * T], lv)
                    tt(mup, mup, halves(e["QH"], lv)[1], ALU.mult)
                    tt(mlo, mlo, halves(e["FH"], lv)[0], ALU.mult)
                v.drain().then_inc(hg_ready, 1)
                for blk in range(9):
                    r, nl, t = (P, 8, P) if blk < BLKS else (TS, 4, TS)
                    v.wait_ge(gram_done, i * 9 + blk + 1)
                    g3 = bank(3 if blk % 2 else 6, nl * P, 0, 0, r).rearrange("p (l t) -> p l t", t=P)[:, :, 0:t]
                    m3 = e["MK"][0:r, 0:nl * P].rearrange("p (l t) -> p l t", t=P)[:, :, 0:t]
                    gm = e["GM"][0:r, 0:nl * P].rearrange("p (l t) -> p l t", t=P)[:, :, 0:t]
                    tt(gm, g3, m3, ALU.mult)
                    v.drain().then_inc(gram_used, 1)
                    v.tensor_reduce(e["SC"][0:r, blk * P:blk * P + t], gm.rearrange("p l t -> p t l"), AX.X, ALU.add)
                    v.drain()
                tt(e["VM"][0:TS, :].rearrange("p (b c) -> p b c", c=P),
                   e["VH"][0:TS, 1024:1152].unsqueeze(1).broadcast_to([TS, NSEQ, P]),
                   bmask.unsqueeze(2).broadcast_to([TS, NSEQ, P]), ALU.mult)
                v.drain().then_inc(vm_ok, 1)
                v.wait_ge(u_done, i + 1)
                ss = lambda c: e["SS"][:, c * P:(c + 1) * P]
                v.tensor_copy(ss(1), bank(6, P))
                for c in range(1, BLKS):
                    v.drain()
                    v.scalar_tensor_tensor(out=ss(c + 1), in0=ss(c), scalar=e["EB"][:, c * P + P - 1:c * P + P],
                                           in1=bank(6, P, c * P), op0=ALU.mult, op1=ALU.add)
                v.drain().then_inc(states_ok, 1)
                v.wait_ge(s0_land, 16 * i + 16)
                v.wait_ge(us_done, i + 1)
                for b in range(NSEQ):
                    at = TP + b * LSEQ + LSEQ - 1
                    v.scalar_tensor_tensor(out=e["SN"][:, b * P:(b + 1) * P], in0=e["S0"][:, b * P:(b + 1) * P],
                                           scalar=e["EB"][:, at:at + 1], in1=bank(3, P, b * P),
                                           op0=ALU.mult, op1=ALU.add)
                v.drain().then_inc(sn_ok, 1)
                v.wait_ge(rinv_ok, i + 1)
                tt(e["QH"], pset(0), e["T1"], ALU.mult)
                v.drain()
                v.scalar_tensor_tensor(out=lo8[:, bass.ds(i * T, T)], in0=e["QH"], scalar=par[:, 248:249],
                                       in1=e["HG"], op0=ALU.mult, op1=ALU.mult)
                v.drain().then_inc(hg_done, 1)
                v.wait_ge(hg_stored, 32 * i + 32)
                v.memset(e["QP"], 0.0)
                v.drain()
                qp = e["QP"].rearrange("p (b j) -> p b j", j=136)
                for c in range(2):
                    rows = slice(64 * c, 64 * c + 64)
                    v.tensor_copy(qp[rows, :, 64 * c:64 * c + 8], seqs(e["DQ"])[rows])
                    v.tensor_copy(qa[rows, 64 * c:64 * c + 64], e["DQ"][rows, TP:T])
                v.drain().then_inc(qp_ok, 1)
                for qb in range(BLKS):
                    n = (qb + 1) * P
                    v.wait_ge(qk_done, i * 8 + qb + 1)
                    for bk in (3, 6):
                        d = bank(bk, P, qb * P)
                        tt(d, d, causal[:, :], ALU.add)
                    v.drain()
                    v.tensor_reduce(small[:, 24:25], bank(3, n), AX.X, ALU.max)
                    v.tensor_reduce(small[:, 25:26], bank(6, n), AX.X, ALU.max)
                    v.drain()
                    v.tensor_scalar(small[:, 26:28], small[:, 24:26], -0.125, None, ALU.mult)
                    v.drain().then_inc(nmax_ok, 1)
                    v.wait_ge(probs_ok, i * 8 + qb + 1)
                    v.reciprocal(small[:, 34:36], small[:, 28:30])
                    v.drain()
                    tt(small[:, 35:36], small[:, 35:36], NLAM, ALU.mult)
                    v.drain()
                    v.tensor_scalar(e["P1"][:, 0:n], e["P1"][:, 0:n], small[:, 35:36], None, ALU.mult)
                    v.drain()
                    v.scalar_tensor_tensor(out=e["P1"][:, 0:n], in0=e["P0"][:, 0:n], scalar=small[:, 34:35],
                                           in1=e["P1"][:, 0:n], op0=ALU.mult, op1=ALU.add)
                    v.drain().then_inc(w_ok, 1)
                for b in range(NSEQ):
                    v.wait_ge(ktr_done, i * 16 + 2 * b + 2)
                    if b:
                        v.wait_ge(sqk_done, i * 16 + 2 * b)
                    v.tensor_copy(e["KTS"][:, 512:1024], bank(7)).then_inc(ktd_ok, 1)
                v.wait_ge(sqk_done, i * 16 + 16)
                tt(bank(5, 64), bank(5, 64), newmask[:, :], ALU.add)
                v.drain()
                v.tensor_reduce(small[:, 30:31], pset(1), AX.X, ALU.max)
                v.drain()
                v.tensor_scalar(small[:, 31:32], small[:, 30:31], -0.125, None, ALU.mult)
                v.drain().then_inc(s_nmax, 1)
                v.wait_ge(s_probs, i + 1)
                v.reciprocal(small[:, 33:34], small[:, 32:33])
                v.drain()
                tt(small[:, 33:34], small[:, 33:34], LAMC, ALU.mult)
                v.drain()
                v.tensor_scalar(qa[:, 0:64], ist[:, :], small[:, 33:34], None, ALU.mult)
                v.drain().then_inc(s_comb, 1)
                v.wait_ge(srinv, i + 1)
                tt(e["P1"], pset(0), e["P0"], ALU.mult)
                v.drain()
                v.tensor_scalar(lo8[:, bass.ds(i * T + 4 * T, T)], e["P1"], par[:, 249:250], 1.0 - LAM_INIT,
                                ALU.mult, ALU.mult)
                v.memset(qa[:, 0:64], 0.0)
                v.drain().then_inc(attn_done, 1)

            def residual(stage, res):
                v.memset(accum[:, 0:T], 0.0)
                trips, jobs, _ = STAGES[stage]
                with v.Fori(0, trips) as i:
                    for j in range(jobs):
                        q, used, n = job(stage, i, j)
                        z = res[:, bass.ds(i * jobs * T + j * T, T)]
                        v.wait_ge(job_done, n + 1)
                        v.scalar_tensor_tensor(out=quads(z), in0=quads(z), scalar=ALPHA, in1=quad(q), op0=ALU.mult,
                                               op1=ALU.add).then_inc(job_free[q], 1)
                        v.drain()
                        tt(accum[:, 0:T], accum[:, 0:T], z, ALU.add)
                v.drain().then_inc(ln_acc, 1)

            def norm(n, src):
                v.wait_ge(ln_mean, n + 1)
                for k in range(KT):
                    v.scalar_tensor_tensor(out=xs(src, k), in0=pset(0), scalar=-1.0 / D, in1=xs(src, k),
                                           op0=ALU.mult, op1=ALU.add).then_inc(ln_xc, 1)
                v.drain()
                v.wait_ge(ln_rstd, n + 1)
                for k in range(KT):
                    tt(xs(src, k), xs(src, k), ln["RSTD"], ALU.mult).then_inc(ln_y, 1)

            def mlp(layer):
                with v.Fori(0, 8) as i:
                    for j in range(4):
                        v.wait_ge(relu_ok, i * 4 + (32 * layer + j + 1))
                        h = big[:, bass.ds(i * 4 * T + j * T, T)]
                        tt(h, h, h, ALU.mult).then_inc(hid_ok, 1)
                residual(f"down{layer}", xa)
                norm(2 * layer + 1, xa)
                with v.Fori(0, 4) as i:
                    for j in range(2):
                        q, used, n = job(f"ple{layer}", i, 2 * j + 1)
                        v.drain()
                        v.wait_ge(gate_ok, i * 2 + (8 * layer + j + 1))
                        v.wait_ge(job_done, n + 1)
                        tt(quads(pl["TMP"]), quads(xs(pl["GATE"], j)), quad(q), ALU.mult).then_inc(job_free[q], 1)
                        v.drain()
                        tt(lo8[:, bass.ds(i * 2 * T + j * T, T)], xa[:, bass.ds(i * 2 * T + j * T, T)],
                           pl["TMP"], ALU.add).then_inc(ple_ct, 1)
                v.drain()

            residual("out", xa)
            norm(0, xa)
            mlp(0)
            last = rows4[3][:, 0:72]
            x3 = lo8.rearrange("p (k t) -> p k t", t=T)
            x4 = x3[:, :, TP:T].rearrange("p k (b s) -> p k b s", s=LSEQ)
            d3 = xa[:, :].rearrange("p (k t) -> p k t", t=T)
            d4 = d3[:, :, TP:T].rearrange("p k (b s) -> p k b s", s=LSEQ)
            v.tensor_copy(last[:, 0:8].unsqueeze(2), x3[:, :, TP - 1:TP])
            v.tensor_copy(last[:, 8:72].rearrange("p (b k) -> p k b", k=8), x4[:, :, :, 7])
            v.drain().then_inc(sg_ok, 1)
            tt(d3[:, :, 1:TP], x3[:, :, 0:TP - 1], x3[:, :, 1:TP], ALU.subtract)
            v.tensor_scalar(d3[:, :, 0:1], x3[:, :, 0:1], -1.0, None, ALU.mult)
            tt(d4[:, :, :, 1:8], x4[:, :, :, 0:7], x4[:, :, :, 1:8], ALU.subtract)
            tt(d4[:, :, :, 0], par[:, P:P + 64].rearrange("p (b k) -> p k b", k=8), x4[:, :, :, 0], ALU.subtract)
            v.drain()
            for n, m in enumerate((1, 4, 5, 0, 2, 3)):
                if n >= 2:
                    v.wait_ge(xm_used, n - 1)
                for k in range(KT):
                    at = 64 + m * 8 + k
                    v.scalar_tensor_tensor(out=xs(mixed[n % 2], k), in0=xs(xa, k), scalar=par[:, at:at + 1],
                                           in1=xs(lo8, k), op0=ALU.mult, op1=ALU.add)
                v.drain().then_inc(xm_ok, 1)

            with v.Fori(0, KT) as i:
                par7 = par[:, 192:248].rearrange("p (n k) -> p n k", k=8)
                v.tensor_copy(cur[:, 0:7].unsqueeze(2), par7[:, :, bass.ds(i, 1)])
                v.drain()
                v.tensor_scalar(cur[:, 7:8], cur[:, 3:4], -1.0, 1.0, ALU.mult, ALU.add)
                v.drain().then_inc(rw_dve, 1)
                v.wait_ge(rw_act, i * 6 + 1)
                v.tensor_scalar(w["LW"], w["LW"], -math.exp(-0.5), None, ALU.mult)
                v.drain()
                v.tensor_tensor_scan(w["C"], reset[:, :], w["LW"], 0.0, ALU.mult, ALU.add)
                v.wait_ge(rkv_land, i * 48 + 48)
                v.tensor_scalar(w["KK"], w["K"], cur[:, 2:3], None, ALU.mult)
                v.drain()
                tt(w["EPP"], w["C"], w["LW"], ALU.subtract)
                v.drain().then_inc(rw_dve, 1)
                v.wait_ge(rw_act, i * 6 + 2)
                v.tensor_scalar(w["LW"], w["SA"], cur[:, 3:4], cur[:, 7:8], ALU.mult, ALU.add)
                v.drain()
                tt(w["K"], w["K"], w["LW"], ALU.mult)
                v.wait_ge(rw_mm, i * 5 + 4)
                v.tensor_scalar(w["RN"], pset(1), 1e-24, 2.0 ** 20, ALU.max, ALU.mult)
                v.drain().then_inc(rw_dve, 1)
                v.scalar_tensor_tensor(out=w["LW"], in0=w["R"], scalar=cur[:, 6:7], in1=w["K"],
                                       op0=ALU.mult, op1=ALU.mult)
                v.drain().then_inc(rw_dve, 1)
                v.wait_ge(rw_act, i * 6 + 5)
                ar, bk = w["AR"], w["BK"]
                tt(ar[:, T:2 * T], w["R"], w["EP"], ALU.mult)
                tt(bk[:, T:2 * T], w["K"], w["C"], ALU.mult)
                v.tensor_copy(small[:, 40:56], w["EP"][:, CH - 1:TP:CH])
                v.tensor_copy(small[:, 56:64], w["EP"][:, TP + 7:T:LSEQ])
                v.wait_ge(rw_act, i * 6 + 6)
                tt(w["KK"], w["KK"], w["RN"], ALU.mult)
                v.drain()
                v.scalar_tensor_tensor(out=ar[:, 0:T], in0=w["KK"], scalar=-1.0, in1=w["EPP"],
                                       op0=ALU.mult, op1=ALU.mult)
                tt(w["SA"], w["KK"], w["SA"], ALU.mult)
                v.drain()
                tt(bk[:, 0:T], w["SA"], w["C"], ALU.mult)
                v.wait_ge(rw_mm, i * 5 + 5)
                tt(w["BON"], pset(0), w["V"], ALU.mult)
                v.drain().then_inc(rw_dve, 1)
                g4 = gmask.rearrange("p (r t) -> p r t", r=2)
                s4 = smask.rearrange("p (r t) -> p r t", r=2)
                for h in range(2):
                    ab = w["AB"].rearrange("p (m t) -> p m t", m=2)
                    rb = w[f"RB{h}"].rearrange("p (m t) -> p m t", m=2)
                    if h:
                        v.wait_ge(akv_done, i * 2 + 1)
                    for blk in range(9):
                        r, t, mk = (P, P, g4) if blk < BLKS else (TS, TS, s4)
                        v.wait_ge(gr_done, i * 18 + h * 9 + blk + 1)
                        g = bank(blk % 4, BANK, 0, 0, r).rearrange("p (m r t) -> p m r t", m=2, r=2)
                        for which, dst in ((0, ab), (1, rb)):
                            last_ = tt(dst[0:r, :, blk * P:blk * P + t], g[:, :, which, 0:t],
                                       mk[:, which:which + 1, :].broadcast_to([r, 2, t]), ALU.mult)
                        v.drain().then_inc(gr_used, 1)
                    xts = w[f"XT{h}"]
                    for t in (w["X"], xts):
                        v.tensor_copy(blocks(t), ident[:, :].unsqueeze(1).broadcast_to([P, BLKS, P]))
                        v.tensor_copy(t[0:64, TP:T], ident[0:64, 0:64])
                    v.drain().then_inc(x_ok, 1)
                    for lv in range(RWL):
                        lm = lmask[:, lv * CH:(lv + 1) * CH]
                        for g in range(2):
                            v.wait_ge(p1_done, (i * 2 + h) * 12 + 2 * lv + g + 1)
                            v3 = lambda t: t.rearrange("p (n c) -> p n c", c=CH)
                            tt(v3(w["P1M"][:, g * 512:g * 512 + 512]), v3(bank(g)),
                               lm.unsqueeze(1).broadcast_to([P, 8, CH]), ALU.mult)
                            if g:
                                tt(w["P1M"][0:64, TP:T], bank(2, 64, 0, 0, 64), lm[0:64], ALU.mult)
                            v.drain().then_inc(p1m_ok, 1)
                        for g in range(2):
                            v.wait_ge(x_done, (i * 2 + h) * 12 + 2 * lv + g + 1)
                            cols = slice(g * 512, g * 512 + 512)
                            tt(xts[:, cols], xts[:, cols], bank(6 + g), ALU.add)
                            if g:
                                tt(xts[0:64, TP:T], xts[0:64, TP:T], bank(5, 64, 64, 0, 64), ALU.add)
                            if lv < RWL - 1:
                                tt(w["X"][:, cols], w["X"][:, cols], bank(3 + g), ALU.add)
                                if g:
                                    tt(w["X"][0:64, TP:T], w["X"][0:64, TP:T], bank(5, 64, 0, 0, 64), ALU.add)
                            v.drain().then_inc(x_ok, 1)
                v.memset(state[:, 0:P], 0.0)
                v.drain().then_inc(st_ok, 1)
                for c in range(NCH):
                    old, new = state[:, c % 2 * P:(c % 2 + 1) * P], state[:, (c + 1) % 2 * P:((c + 1) % 2 + 1) * P]
                    v.wait_ge(st_mm, i * 16 + c + 1)
                    tt(new, old, bank(6 + c % 2, P), ALU.add)
                    v.drain()
                    v.scalar_tensor_tensor(out=new, in0=new, scalar=small[:, 40 + c:41 + c], in1=headones[:, :],
                                           op0=ALU.mult, op1=ALU.mult)
                    v.drain().then_inc(st_ok, 1)
                    if c == 0:
                        v.wait_ge(tat_ok, i + 1)
                        v.memset(w["TATM"], 0.0)
                        v.drain()
                        tm = w["TATM"].rearrange("p (b j) -> p b j", j=72)
                        v.tensor_copy(tm[:, :, 0:8], seqs(w["TAT"]))
                        tt(w["VM"][0:TS, :].rearrange("p (b c) -> p b c", c=P),
                           w["VTK"][0:TS, 1024:1152].unsqueeze(1).broadcast_to([TS, NSEQ, P]),
                           bmask.unsqueeze(2).broadcast_to([TS, NSEQ, P]), ALU.mult)
                        v.drain().then_inc(tatm_ok, 1)
                v.wait_ge(us_cp, i * 17 + 17)
                tt(w["USM"][0:TS, :].rearrange("p (b c) -> p b c", c=P),
                   w["US"][0:TS, 1024:1152].unsqueeze(1).broadcast_to([TS, NSEQ, P]),
                   bmask.unsqueeze(2).broadcast_to([TS, NSEQ, P]), ALU.mult)
                v.drain().then_inc(usm_ok, 1)
                v.wait_ge(sst_mm, i + 1)
                st3 = w["ST0"].rearrange("p (b c) -> p b c", c=P)
                tt(w["ST0"], w["ST0"], bank(6, 1024), ALU.add)
                v.drain()
                tt(st3, st3, small[:, 56:64].unsqueeze(2).broadcast_to([P, 8, P]), ALU.mult)
                v.drain()
                tt(st3, st3, headones[:, :].unsqueeze(1).broadcast_to([P, 8, P]), ALU.mult)
                v.drain().then_inc(sst_ok, 1)
                v.wait_ge(gn_mm, i * 2 + 1)
                v.scalar_tensor_tensor(out=w["YS"], in0=pset(0), scalar=-1.0 / 64, in1=w["YS"],
                                       op0=ALU.mult, op1=ALU.add)
                v.drain().then_inc(gn_dve, 1)
                v.wait_ge(gn_act, i * 2 + 2)
                tt(w["YS"], w["YS"], w["RS"], ALU.mult)
                v.drain()
                v.tensor_scalar(w["YS"], w["YS"], cur[:, 4:5], cur[:, 5:6], ALU.mult, ALU.add)
                v.drain()
                tt(w["YS"], w["YS"], w["BON"], ALU.add)
                v.drain()
                tt(xa[:, bass.ds(i * T, T)], w["YS"], w["GT"], ALU.mult)
                v.drain().then_inc(gn_dve, 1)
                v.drain().then_inc(rw_out, 1)
            residual("rout", lo8)
            norm(2, lo8)
            mlp(1)
            for b in range(1, 9, 2):
                v.wait_ge(y_tr, b + 1)
                v.wait_ge(y_rows, b)
                v.tensor_copy(yout[:, b * D:(b + 1) * D], bank(b % 4 * 2, D))
                v.drain().then_inc(y_rows, 1)

        @block.tensor
        def _(pe):
            def mm(out, lhsT, rhs, start=True, stop=True):
                return pe.matmul(out, lhsT, rhs, start=start, stop=stop, skip_group_check=True)

            for s in range(SLOTS):
                pe.drain().then_inc(w_used[s], 1)
            pe.wait_ge(consts, 1)
            pe.wait_ge(in_rows, 16 * 16)
            pe.transpose(bank(6, 112), prow[0:112, 0:P], ident[0:112, 0:112])
            pe.transpose(bank(6, 126, P), prow[0:126, P:2 * P], ident[0:126, 0:126]).then_inc(par_tr, 1)
            pe.wait_ge(in_x, 32)
            for k in range(KT):
                if k >= 2:
                    pe.wait_ge(xt_copied, k - 1)
                for b in range(9):
                    n = P if b < BLKS else TS
                    last = pe.transpose(pset(k % 2, b * P, n), xin[0:n, b * D + k * P:b * D + (k + 1) * P],
                                        ident[0:n, 0:n])
                last.then_inc(xt_done, 1)
            pe.wait_ge(xt_copied, KT)

            def project(stage, i, j, units, rhs, kts=KT, m=P, row=0, width=P):
                q, used, _ = job(stage, i, j)
                pe.wait_ge(job_free[q], used + 1)
                spans = [(pset(q, lo, n), lo, n) for lo, n in SPANS] if stage == "in" else [
                    (quad(q, row, row + m)[:, b, :], b * QUAD, QUAD) for b in range(4)]
                n_units = len(units)
                for g, u in enumerate(units):
                    slot, before_ = unit(stage, i, u)
                    pe.wait_ge(w_land[slot], before_ * 16 + 16)
                    for k in range(kts):
                        for out, lo, n in spans:
                            last = mm(out, ring[:, slot * 1024 + k * width:slot * 1024 + k * width + m],
                                      xs(rhs, g * KT + k, lo, n), g == 0 and k == 0,
                                      g == n_units - 1 and k == kts - 1)
                    last.then_inc(w_used[slot], 1)
                pe.drain().then_inc(job_done, 1)

            def project_rows(stage, i, j, u, lhs):
                q, used, _ = job(stage, i, j)
                pe.wait_ge(job_free[q], used + 1)
                slot, before_ = unit(stage, i, u)
                pe.wait_ge(w_land[slot], before_ * 16 + 16)
                for b in range(9):
                    n = P if b < BLKS else TS
                    for k in range(KT):
                        last = mm(pset(q, b * P, P, 0, n), xs(lhs, k, b * P, n),
                                  ring[:, slot * 1024 + k * P:slot * 1024 + (k + 1) * P], k == 0, k == KT - 1)
                last.then_inc(w_used[slot], 1)
                pe.drain().then_inc(job_done, 1)

            def wide(q, lhsT, rhs):
                for lo, n in SPANS:
                    last = mm(pset(q, lo, n), lhsT, rhs[:, lo:lo + n])
                return last

            def rows_of(q, src):
                for b in range(9):
                    n = P if b < BLKS else TS
                    last = pe.transpose(pset(q, b * P, P, 0, n), src[:, b * P:b * P + n], ident[:, :])
                return last

            with pe.Fori(0, HEADS) as i:
                for j in range(7):
                    if j in (3, 6):
                        project_rows("in", i, j, j, xa)
                    else:
                        project("in", i, j, [j], xa)
                pe.wait_ge(in_evac, i * 7 + 7)
                pe.wait_ge(hg_ready, i + 1)
                ml = e["ML"]
                for blk in range(9):
                    n, nl = (P, 8) if blk < BLKS else (TS, 4)
                    bk = 3 if blk % 2 else 6
                    if blk >= 2:
                        pe.wait_ge(gram_used, i * 9 + blk - 1)
                    for lv in range(nl):
                        at = (lv - 1) * T + blk * P
                        lhsT = e["FH"][:, blk * P:blk * P + n] if lv == 0 else ml[:, at:at + n]
                        rhs = e["QH"][:, blk * P:blk * P + n] if lv == 0 else ml[:, at:at + n]
                        last = mm(bank(bk, n, lv * P, 0, n), lhsT, rhs)
                    last.then_inc(gram_done, 1)
                pe.wait_ge(gram_used, i * 9 + 8)
                rows_of(1, e["T1"]).then_inc(kdt_done, 1)
                pe.wait_ge(gram_used, i * 9 + 9)
                pe.wait_ge(kdt_ok, i + 1)
                for c in range(BLKS):
                    last = mm(bank(6, P, c * P), e["KDT"][:, c * P:(c + 1) * P], e["VH"][:, c * P:(c + 1) * P])
                last.then_inc(u_done, 1)
                pe.wait_ge(vm_ok, i + 1)
                for g in range(2):
                    last = mm(bank(3 + g), e["KDT"][0:TS, 1024:1152], e["VM"][0:TS, g * 512:(g + 1) * 512])
                last.then_inc(us_done, 1)
                pe.wait_ge(states_ok, i + 1)
                pe.wait_ge(s0_land, 16 * i + 16)
                for c in range(BLKS):
                    o_ = pset(0, c * P, P)
                    last = mm(o_, e["VH"][:, c * P:(c + 1) * P], e["SC"][:, c * P:(c + 1) * P], True, c == 0)
                    if c:
                        last = mm(o_, e["SS"][:, c * P:(c + 1) * P], e["QB"][:, c * P:(c + 1) * P], False, True)
                mm(pset(0, TP, TS), e["VH"][0:TS, 1024:1152], e["SC"][0:TS, TP:T], True, False)
                for b in range(NSEQ):
                    at = TP + b * LSEQ
                    last = mm(pset(0, at, LSEQ), e["S0"][:, b * P:(b + 1) * P], e["QB"][:, at:at + LSEQ],
                              False, b == NSEQ - 1)
                last.then_inc(o_done, 1)
                pe.wait_ge(o_sq, i + 1)
                pe.wait_ge(sn_ok, i + 1)
                wide(1, ones[:, :], e["QH"]).then_inc(ss_done, 1)
                pe.wait_ge(rinv_ok, i + 1)
                rows_of(1, e["DK"]).then_inc(ko_done, 1)
                pe.wait_ge(ko_ok, i + 1)
                pe.wait_ge(hg_done, i + 1)

                def scores(qb):
                    if qb:
                        pe.wait_ge(probs_ok, i * 8 + qb)
                    n = (qb + 1) * P
                    for c, bk in ((0, 3), (1, 6)):
                        rows = slice(64 * c, 64 * c + 64)
                        for lo in range(0, n, BANK):
                            m = min(BANK, n - lo)
                            last = mm(bank(bk, m, lo), e["DQ"][rows, qb * P:(qb + 1) * P], e["DK"][rows, lo:lo + m])
                    last.then_inc(qk_done, 1)

                scores(0)
                for qb in range(BLKS):
                    if qb + 1 < BLKS:
                        scores(qb + 1)
                    pe.wait_ge(w_ok, i * 8 + qb + 1)
                    done = qb if qb < 5 else 2 * qb - 4
                    for g in range(1 if qb < 4 else 2):
                        if qb or g:
                            pe.wait_ge(wt_ok, i * 12 + done + g)
                        for n in range(4 * g, min(4 * g + 4, qb + 1)):
                            last = pe.transpose(bank(5, P, (n - 4 * g) * P), e["P1"][:, n * P:(n + 1) * P], ident[:, :])
                        last.then_inc(wtr_done, 1)
                    pe.wait_ge(wt_ok, i * 12 + done + (1 if qb < 4 else 2))
                    for n in range(qb + 1):
                        last = mm(pset(0, qb * P, P), e["DV"][:, n * P:(n + 1) * P], e["WT"][:, n * P:(n + 1) * P],
                                  n == 0, n == qb)
                    last.then_inc(pv_done, 1)
                pe.wait_ge(qp_ok, i + 1)

                def landed(n):
                    s = n % 3
                    per = len(range(s, 16, 3))
                    for land in (kv_land[s], kv_odd_land[s]):
                        pe.wait_ge(land, i * (64 * per) + 64 * (n // 3 + 1))
                    return e["KV"][:, s * 1024:(s + 1) * 1024]

                for b in range(NSEQ):
                    kv = landed(b)
                    for g in range(2):
                        if b:
                            pe.wait_ge(kta_ok if g == 0 else ktd_ok, i * 8 + b)
                        for n in range(4):
                            last = pe.transpose(bank(6 + g, P, n * P), kv[:, (4 * g + n) * P:(4 * g + n + 1) * P],
                                                ident[:, :])
                        last.then_inc(ktr_done, 1)
                    pe.drain().then_inc(kv_used, 1)
                    for g in range(2):
                        pe.wait_ge(kta_ok if g == 0 else ktd_ok, i * 8 + b + 1)
                        last = mm(bank(3 + g), e["QP"][:, b * P:(b + 1) * P], e["KTS"][:, g * 512:(g + 1) * 512],
                                  b == 0, b == NSEQ - 1)
                        if b == NSEQ - 1 and g == 1:
                            last = mm(bank(5, 64), qa[:, :], e["DK"][:, TP:T])
                        last.then_inc(sqk_done, 1)
                pe.wait_ge(s_comb, i + 1)
                for n in range(9):
                    m = P if n < BLKS else TS
                    last = mm(bank(6, 64, n * 64, 0, m), e["P0"][:, n * P:n * P + m], qa[:, 0:64])
                last.then_inc(swt_done, 1)
                pe.wait_ge(swt_ok, i + 1)
                mm(pset(0, TP, TS), e["DV"][0:TS, 1024:1152], e["WTS"][0:TS, 512:576], True, False)
                for b in range(NSEQ):
                    kv = landed(NSEQ + b)
                    for g in range(PAGES):
                        at = TP + b * LSEQ
                        last = mm(pset(0, at, LSEQ), kv[:, g * P:(g + 1) * P],
                                  e["WTS"][:, g * 64 + b * 8:g * 64 + b * 8 + 8], False, b == 7 and g == 7)
                    last.then_inc(kv_used, 1)
                pe.drain().then_inc(so_done, 1)
                pe.wait_ge(so_sq, i + 1)
                wide(1, ones[:, :], e["P1"]).then_inc(sss_done, 1)
                pe.wait_ge(attn_done, i + 1)

            def square(stage, rhs):
                with pe.Fori(0, 2) as i:
                    for j in range(4):
                        project(stage, i, j, [j], rhs)

            def norm(n):
                pe.wait_ge(ln_acc, n + 1)
                wide(0, ones[:, :], accum).then_inc(ln_mean, 1)
                pe.wait_ge(ln_sqsum, 8 * n + 8)
                wide(1, ones[:, :], ln["VACC"]).then_inc(ln_var, 1)
                pe.wait_ge(ln_done, 8 * n + 8)

            def mlp(layer):
                with pe.Fori(0, 8) as i:
                    for j in range(4):
                        project(f"up{layer}", i, j, [j], xa)
                pe.wait_ge(hid_ok, 32 * layer + 32)
                with pe.Fori(0, 4) as i:
                    for j in range(2):
                        project(f"down{layer}", i, j, [4 * j + g for g in range(4)], big)
                norm(2 * layer + 1)
                pe.wait_ge(p_land, 32 * layer + 32)
                for k in range(2):
                    for b in range(9):
                        n = P if b < BLKS else TS
                        last = pe.transpose(pset(k, b * P, n),
                                            pl["ROWS"][0:n, b * PLE + k * P:b * PLE + (k + 1) * P], ident[0:n, 0:n])
                    last.then_inc(pt_tr, 1)
                pe.wait_ge(pt_ok, layer + 1)
                with pe.Fori(0, 4) as i:
                    for j in range(2):
                        project(f"ple{layer}", i, 2 * j, [2 * j], xa)
                        project(f"ple{layer}", i, 2 * j + 1, [2 * j + 1], pl["PT"], kts=2)

            square("out", lo8)
            norm(0)
            mlp(0)
            pe.wait_ge(sg_ok, 1)
            pe.transpose(bank(7, P, QUAD, 0, 72), rows4[3][:, 0:72], ident[:, :]).then_inc(sg_tr, 1)
            pe.wait_ge(xm_ok, 1)
            project("lora", 0, 0, [0], mixed[0], m=64, width=64)
            pe.drain().then_inc(xm_used, 1)
            pe.wait_ge(xm_ok, 2)
            pe.wait_ge(sg_rows, 1)
            project("lora", 0, 1, [1], mixed[1], m=64, row=64, width=64)
            pe.drain().then_inc(xm_used, 1)
            pe.wait_ge(xm_ok, 3)
            project("lora", 0, 2, [2], mixed[0])
            project("lora", 0, 3, [3], mixed[0], m=32, width=32)
            pe.drain().then_inc(xm_used, 1)
            for n, name in enumerate("rkv"):
                pe.wait_ge(xm_ok, 4 + n)
                square(name, mixed[(n + 1) % 2])
                pe.drain().then_inc(xm_used, 1)

            pe.wait_ge(lora_ok, 1)
            for q, s in ((0, "v"), (1, "v")):
                used = job("rout", 0, q)[1]
                pe.wait_ge(job_free[q], used + 1)
            pe.wait_ge(rw_masks, 1)
            with pe.Fori(0, KT) as i:
                pe.wait_ge(lora2_land, i * 64 + 64)
                for lo, n in SPANS:
                    last = mm(pset(0, lo, n), lora2[0:64, 0:P], hid_wa[0:64, lo:lo + n])
                last.then_inc(rw_mm, 1)
                for lo, n in SPANS:
                    last = mm(pset(1, lo, n), lora2[64:P, 0:P], hid_wa[64:P, lo:lo + n])
                last.then_inc(rw_mm, 1)
                pe.wait_ge(rw_act, i * 6 + 1)
                for lo, n in SPANS:
                    mm(pset(0, lo, n), lora2[:, P:2 * P], hid_g1[:, lo:lo + n], True, False)
                    last = mm(pset(0, lo, n), lora2[0:32, 2 * P:3 * P], hid_g2[0:32, lo:lo + n], False, True)
                last.then_inc(rw_mm, 1)
                pe.wait_ge(rw_act, i * 6 + 4)
                wide(1, headones[:, :], w["RN"]).then_inc(rw_mm, 1)
                pe.wait_ge(rw_dve, i * 5 + 4)
                wide(0, headones[:, :], w["LW"]).then_inc(rw_mm, 1)
                pe.wait_ge(rw_dve, i * 5 + 5)
                for n, src in enumerate((w["AR"][:, 0:T], w["BK"][:, 0:T], w["BK"][:, T:2 * T], w["V"])):
                    if n >= 2:
                        pe.wait_ge(rw_trc, i * 4 + n - 1)
                    rows_of((n + 1) % 2, src).then_inc(rw_tr, 1)
                pe.wait_ge(rw_trc, i * 4 + 4)
                for h in range(2):
                    rows = slice(64 * h, 64 * h + 64)
                    xts = w[f"XT{h}"]
                    if h:
                        pe.wait_ge(akv_ok, i * 2 + 1)
                    arv = w["AR"].rearrange("p (m t) -> p m t", m=2)
                    for blk in range(9):
                        n = P if blk < BLKS else TS
                        at = h * 9 + blk
                        if blk >= 4:
                            pe.wait_ge(gr_used, i * 18 + at - 3)
                            if blk == BLKS:
                                pe.sem_inc(passed, 1)
                        for m in range(2):
                            g = bank(blk % 4, 256, m * 256, 0, n).rearrange("p (r t) -> p r t", r=2)[:, :, 0:n]
                            last = mm(g, w["BK"][rows, m * T + blk * P:m * T + blk * P + n],
                                      arv[rows, :, blk * P:blk * P + n])
                        last.then_inc(gr_done, 1)
                    pe.wait_ge(gr_used, i * 18 + h * 9 + 9)
                    pe.wait_ge(x_ok, (i * 2 + h) * 13 + 1)
                    groups = ((0, 1, 2, 3), (4, 5, 6, 7, 8))

                    def place(first, blk):
                        n = P if blk < BLKS else TS
                        if blk == BLKS:
                            return {0: bank(2, n, 0, 0, n), 3: bank(5, n, 0, 0, n), 6: bank(5, n, 64, 0, n)}[first]
                        return bank(first + blk // 4, P, blk % 4 * P)

                    def tile_(t, blk):
                        n = P if blk < BLKS else TS
                        return t[0:n, blk * P:blk * P + n]

                    for lv in range(RWL):
                        for g in range(2):
                            if lv:
                                pe.wait_ge(x_ok, (i * 2 + h) * 13 + 2 * lv + g)
                            for blk in groups[g]:
                                last = mm(place(0, blk), tile_(w["AB"], blk), tile_(w["X"], blk))
                            last.then_inc(p1_done, 1)
                        for g in range(2):
                            pe.wait_ge(p1m_ok, (i * 2 + h) * 12 + 2 * lv + g + 1)
                            for blk in groups[g]:
                                last = mm(place(6, blk), tile_(w["P1M"], blk), tile_(xts, blk))
                                if lv < RWL - 1:
                                    last = mm(place(3, blk), tile_(xts, blk), tile_(w["P1M"], blk))
                            last.then_inc(x_done, 1)
                    for blk in range(9):
                        n = P if blk < BLKS else TS
                        last = mm(bank(0, 64, blk * 64, 0, n), w["AB"][0:n, T + blk * P:T + blk * P + n],
                                  w["VTK"][0:n, blk * P + 64 * h:blk * P + 64 * h + 64])
                    last.then_inc(akv_done, 1)
                    pe.wait_ge(x_ok, (i * 2 + h) * 13 + 13)
                pe.wait_ge(akv_ok, i * 2 + 2)
                for h in range(2):
                    for blk in range(9):
                        n = P if blk < BLKS else TS
                        last = mm(pset(1, blk * P, n, 64 * h, 64 * h + 64),
                                  w["ATK"][0:n, blk * P + 64 * h:blk * P + 64 * h + 64], tile_(w[f"XT{h}"], blk))
                last.then_inc(tat_done, 1)
                pe.drain().then_inc(rkv_used, 1)
                pe.wait_ge(ws_land, i * 32 + 32)
                for b in range(NSEQ):
                    last = pe.transpose(bank(6, P, b * P), w["WS"][:, b * P:(b + 1) * P], ident[:, :])
                last.then_inc(ws_tr, 1)
                pe.wait_ge(tat_ok, i + 1)
                pe.wait_ge(ws_ok, i + 1)

                def u_rest(c, r, blk, stop_last=True):
                    for h in range(2):
                        last = mm(bank(3 + c % 2, 64, 64 * h, r, r + 64),
                                  w[f"XT{h}"][r:r + 64, blk * P + r:blk * P + r + 64],
                                  w["AKV"][r:r + 64, h * 576 + blk * 64:h * 576 + blk * 64 + 64], False, h == 1)
                    return last

                def y_rest(r, blk, lo):
                    for h in range(2):
                        out = pset(0, lo, 64, 64 * h, 64 * h + 64)
                        rb = w[f"RB{h}"]
                        vc = slice(blk * P + 64 * h, blk * P + 64 * h + 64)
                        tc = blk * P + r
                        mm(out, w["US"][r:r + 64, vc], rb[r:r + 64, tc:tc + 64], False, False)
                        last = mm(out, w["VTK"][r:r + 64, vc], rb[r:r + 64, T + tc:T + tc + 64], False, h == 1)
                    return last

                for c in range(NCH):
                    r, blk = c % 2 * 64, c // 2
                    st = state[:, c % 2 * P:(c % 2 + 1) * P]
                    pe.wait_ge(st_ok, i * 17 + c + 1)
                    mm(bank(3 + c % 2, P, 0, r, r + 64), w["TAT"][:, c * CH:(c + 1) * CH], st, True, False)
                    u_rest(c, r, blk).then_inc(us_mm, 1)
                    mm(pset(0, c * CH, CH), st, w["AR"][:, T + c * CH:T + (c + 1) * CH], True, False)
                    pe.wait_ge(us_cp, i * 17 + c + 1)
                    mm(bank(6 + c % 2, P), w["BTK"][r:r + 64, blk * P:(blk + 1) * P],
                       w["US"][r:r + 64, blk * P:(blk + 1) * P], True, False)
                    mm(bank(6 + c % 2, P), w["KTK"][r:r + 64, blk * P:(blk + 1) * P],
                       w["VTK"][r:r + 64, blk * P:(blk + 1) * P], False, True).then_inc(st_mm, 1)
                    y_rest(r, blk, c * CH)
                pe.wait_ge(tatm_ok, i + 1)
                for b in range(NSEQ):
                    mm(bank(3, P, 0, 0, 64), w["TATM"][:, b * 64:b * 64 + 64], w["ST0"][:, b * P:(b + 1) * P],
                       b == 0, False)
                u_rest(NCH, 0, BLKS).then_inc(us_mm, 1)
                pe.wait_ge(st_ok, i * 17 + 17)
                pe.wait_ge(usm_ok, i + 1)
                for g in range(2):
                    mm(bank(6 + g), w["BTK"][0:TS, 1024:1152], w["USM"][0:TS, g * 512:(g + 1) * 512], True, False)
                    last = mm(bank(6 + g), w["KTK"][0:TS, 1024:1152], w["VM"][0:TS, g * 512:(g + 1) * 512], False, True)
                for b in range(NSEQ):
                    at = TP + b * LSEQ
                    last = mm(pset(0, at, LSEQ), w["ST0"][:, b * P:(b + 1) * P], w["AR"][:, T + at:T + at + LSEQ],
                              b == 0, False)
                last.then_inc(sst_mm, 1)
                y_rest(0, BLKS, TP).then_inc(y_done, 1)
                pe.wait_ge(sst_ok, i + 1)
                for b in range(NSEQ):
                    pe.transpose(pset(1, b * P, P), w["ST0"][:, b * P:(b + 1) * P], ident[:, :])
                pe.transpose(pset(1, 8 * P, P), state[:, 0:P], ident[:, :]).then_inc(so_tr, 1)
                pe.wait_ge(y_ok, i + 1)
                wide(0, headones[:, :], w["YS"]).then_inc(gn_mm, 1)
                pe.wait_ge(gn_act, i * 2 + 1)
                wide(0, headones[:, :], w["SQ"]).then_inc(gn_mm, 1)
                pe.wait_ge(so_ok, i + 1)
                pe.wait_ge(gn_act, i * 2 + 2)
            pe.wait_ge(rw_out, KT)

            square("rout", xa)
            norm(2)
            mlp(1)
            pe.wait_ge(ple_ct, 2 + 2 * KT)
            for b in range(9):
                n = P if b < BLKS else TS
                if b >= 4:
                    pe.wait_ge(y_rows, b - 3)
                for k in range(KT):
                    last = pe.transpose(bank(b % 4 * 2, P, k * P, 0, n), xs(lo8, k, b * P, n), ident[:, :])
                last.then_inc(y_tr, 1)


INPUTS = ["x_prompt", "x_sample", "cache_k", "cache_v", "state_hgrn", "state_wkv", "state_shift", "page_table",
          "p_prompt", "p_sample", "w_in_even", "w_out_even", "hg_lb_logits", "hg_norm_g",
          "da_lam_q1", "da_lam_k1", "da_lam_q2", "da_lam_k2", "da_norm_g",
          "rw_mix", "rw_w_r", "rw_w_k", "rw_w_v", "rw_w_o", "rw_w0", "rw_w1", "rw_w2",
          "rw_a0", "rw_a1", "rw_a2", "rw_g1", "rw_g2",
          "rw_k_k", "rw_k_a", "rw_r_k", "rw_lnx_g", "rw_lnx_b",
          "ln1_g", "ln1_b", "ln2_g", "ln2_b", "mlp_up", "mlp_down", "ple_proj", "ple_gate"]
OUTPUTS = [("y_prompt", (1, TP, D)), ("y_sample", (NSEQ, LSEQ, D)),
           ("k_prompt", (1, 1, TP, HEADS, 2, 64)), ("v_prompt", (1, 1, TP, HEADS, P)),
           ("k_sample", (1, NSEQ, LSEQ, HEADS, 2, 64)), ("v_sample", (1, NSEQ, LSEQ, HEADS, P)),
           ("hgrn_prompt", (1, 1, HEADS, P, P)), ("hgrn_sample", (1, NSEQ, HEADS, P, P)),
           ("wkv_prompt", (1, 1, 16, 64, 64)), ("wkv_sample", (1, NSEQ, 16, 64, 64)),
           ("shift_prompt", (1, 1, D)), ("shift_sample", (1, NSEQ, D))]


def kernel(**inputs):
    import numpy as _np
    import concourse.bacc as _bacc
    from concourse import mybir as _mybir
    from concourse.bass_utils import run_bass_kernel_spmd as _run

    nc = _bacc.Bacc("TRN2", target_bir_lowering=False, num_devices=1)
    arrays, ins, outs = {}, {}, {}
    for name in INPUTS:
        v = _np.ascontiguousarray(inputs[name])
        arrays["in_" + name] = v
        ins[name] = nc.dram_tensor("in_" + name, v.shape, _mybir.dt.from_np(v.dtype), kind="ExternalInput").ap()
    for name, shape in OUTPUTS:
        outs[name] = nc.dram_tensor("out_" + name, shape, F32, kind="ExternalOutput").ap()
    trunk_program(nc, ins, outs)
    r = _run(nc, [arrays], core_ids=[0])
    return tuple(r.results[0]["out_" + name] for name, _ in OUTPUTS)
```

```python
import math
from contextlib import ExitStack

import concourse.bass as bass
from concourse import mybir

F32 = mybir.dt.float32
F32R = mybir.dt.float32r
BF16 = mybir.dt.bfloat16
I32 = mybir.dt.int32
ALU = mybir.AluOpType
ACT = mybir.ActivationFunctionType
AX = mybir.AxisListType

P = 128
D = 1024
KT = D // P
TP = 1024
NSEQ, LSEQ = 8, 8
TS = NSEQ * LSEQ
T = TP + TS
BLKS = TP // P
HEADS = 4
FF = 4 * D
PLE = 256
PAGES = 8
PAGE = 128
ALPHA = 4.0 ** 0.25
LAM_INIT = 0.8 - 0.6
SPANS = [(0, 512), (512, 512), (1024, TS)]
QUAD = T // 4
SLOTS = 6
BANK = 512
NEG = -1e30
LEVELS = 7
KV_SLOTS = 5
CH = 64
NCH = TP // CH
RWL = 6

STAGES = {
    "in": (4, 7, 7), "out": (2, 4, 4),
    "mlp0": (4, 16, 16), "ple0": (4, 4, 4),
    "lora": (1, 4, 4), "r": (2, 4, 4), "k": (2, 4, 4), "v": (2, 4, 4),
    "rout": (2, 4, 4),
    "mlp1": (4, 16, 16), "ple1": (4, 4, 4),
}


def before(stage, count):
    total = 0
    for name, sizes in STAGES.items():
        if name == stage:
            return total
        total += count(name, *sizes)


def in_slot(stage, slot, units):
    slots = 2 if stage.startswith("mlp") else SLOTS
    return len(range(slot, units, slots)) if slot < slots else 0


def unit(stage, i, u):
    _, _, per = STAGES[stage]
    slots = 2 if stage.startswith("mlp") else SLOTS
    slot = u % slots
    base = before(stage, lambda s, t, j, n: t * in_slot(s, slot, n))
    return slot, i * in_slot(stage, slot, per) + (base + u // slots)


def job(stage, i, j):
    _, per, _ = STAGES[stage]
    q = j % 2
    in_trip = len(range(q, per, 2))
    base = before(stage, lambda s, t, n, u: t * len(range(q, n, 2)))
    return q, i * in_trip + (base + j // 2), i * per + (before(stage, lambda s, t, n, u: t * n) + j)


def trunk_program(nc, a, o):
    with ExitStack() as ctx:
        def sb(name, cols, dt=F32, rows=P):
            return ctx.enter_context(nc.sbuf_tensor(name, [rows, cols], dt))

        def sem(name):
            return ctx.enter_context(nc.semaphore(name))

        xa = sb("xa", KT * T)
        with nc.sbuf_tensor("parts", [P, 32 * T], F32R) as parts, nc.sbuf_tensor("wparts", [P, SLOTS * 1024], F32R) as wparts:
            pass
        big = sb("big", 32 * T)
        ring = sb("ring", SLOTS * 1024)
        ident = sb("ident", P)
        ones = sb("ones", P)
        headones = sb("headones", P)
        ist = sb("ist", 64)
        par = sb("par", 256)
        causal = sb("causal", P)
        newmask = sb("newmask", 64)
        cst = sb("cst", 16)
        cur = sb("cur", 16)
        small = sb("small", 64)
        qa = sb("qa", P)
        reset = sb("reset", T, BF16)
        state = sb("state", 2 * P)
        accum = sb("accum", 1152)
        lora2 = sb("lora2", 3 * P)
        pages = ctx.enter_context(nc.sbuf_tensor("pages", [1, NSEQ * PAGES], I32))
        ps = ctx.enter_context(nc.psum_tensor("ps", [P, 8 * BANK], F32))

        EPS_LN, EPS_RMS, EPS_GN, TEN_LN2, NLAM, LAMC = (cst[:, n:n + 1] for n in range(6))

        def xs(t, k, lo=0, n=T):
            return t[:, k * T + lo:k * T + lo + n]

        def blocks(t, width=P):
            return t[:, 0:BLKS * width].rearrange("p (n c) -> p n c", c=width)

        def carve(start, sizes, of=None):
            of = big if of is None else of
            got, at = {}, start
            for name, cols in sizes:
                got[name] = of[:, at:at + cols]
                at += cols
            return got

        e = carve(KT * T, [("QH", T), ("GH", T), ("HG", T), ("T1", T),
                           ("FH", T), ("QB", T), ("EB", T), ("ML", LEVELS * T),
                           ("VH", 1152), ("SC", T), ("GM", 1024), ("S0", 1024),
                           ("DQ", T), ("DK", T), ("DV", 1152), ("RM", T), ("MK", 1024), ("KO", 1152)])
        e.update(carve((KT + 7) * T, [("SS", 1152), ("KDT", 1152), ("VM", 1024), ("SN", 1024)]))
        e.update(carve((KT + 4) * T, [("P0", T), ("P1", T), ("WT", 1024), ("QP", T), ("KV", 3 * 1024),
                                      ("KTS", 1024), ("WTS", 576)]))
        lo8 = big[:, 0:KT * T]
        mixed = [big[:, KT * T:2 * KT * T], big[:, 2 * KT * T:3 * KT * T]]
        xin = big[:, 0:9 * D]
        prow = e["SC"][:, 0:256]
        lamv = e["GM"][:, 0:256]
        pl = carve(8 * T, [("ROWS", 9 * PLE), ("PT", 2 * T), ("GATE", 2 * T), ("TMP", T)])
        x_hi, x_lo, h_hi, h_lo = (parts[:, n * KT * T:(n + 1) * KT * T] for n in range(4))
        w_hi, w_lo = ([wparts[:, (2 + 2 * q + n) * 1024:(3 + 2 * q + n) * 1024] for q in range(2)] for n in range(2))
        hidden = accum[:, 0:T]
        z_scale = cst[:, 6:7]
        ln = carve(24 * T, [(f"SQ{k}", T) for k in range(KT)])
        ln["RSTD"] = ln["SQ0"]
        yout = big[:, KT * T:KT * T + 9 * D]
        hid_wa, hid_g1, hid_g2, rwm = (big[:, (24 + n) * T:(25 + n) * T] for n in range(4))
        gmask = rwm[:, 0:256]
        smask = rwm[0:64, 256:384]
        lmask = rwm[:, 384:384 + RWL * CH]
        umask = rwm[:, 768:832]
        bmask = cst[0:64, 8:16]
        rows4 = [big[:, (28 + n) * T:(29 + n) * T] for n in range(4)]
        w = carve(8 * T, [("R", T), ("K", T), ("V", T), ("GT", T), ("BON", T), ("AR", 2 * T), ("BK", 2 * T),
                          ("LW", T), ("C", T), ("EPP", T), ("EP", T), ("KK", T), ("RN", T), ("SA", T)])
        w.update(carve(28 * T, [("KTK", 1152), ("VTK", 1152), ("WS", 1024), ("ST0", 1024)]))
        w.update(carve(8 * T, [("AB", 2 * T)]))
        w.update(carve(17 * T, [("X", T), ("P1M", T), ("XT0", T), ("XT1", T), ("TAT", T), ("AKV", 1152)]))
        w.update(carve(17 * T, [("US", 1152)]))
        w.update(carve(0, [("RB0", 2 * T), ("RB1", 2 * T), ("ATK", 1152)], ring))
        w["BTK"] = accum
        w["TATM"], w["USM"], w["VM"] = w["AR"][:, 0:576], w["BK"][:, 0:1024], w["BK"][:, T:T + 1024]
        w["YS"], w["SQ"], w["RS"], w["SO"] = w["XT0"], w["XT1"], w["TAT"], w["ATK"]

        w_land = [sem(f"w_land{s}") for s in range(SLOTS)]
        w_used = [sem(f"w_used{s}") for s in range(SLOTS)]
        job_done = sem("job_done")
        job_free = [sem(f"job_free{q}") for q in range(2)]
        (in_rows, in_x, in_misc, consts, par_tr, par_ok, xt_done, xt_copied, lam_ok,
         in_evac, hg_pre, hg_exp, hg_ready, gram_done, gram_used, kdt_done, kdt_ok, vm_ok, u_done, us_done,
         states_ok, sn_ok, s0_land, o_done, o_sq, ss_done, rinv_ok, hg_done, hg_stored,
         ko_done, ko_ok, kv_stored, qp_ok, qk_done, nmax_ok, probs_ok, w_ok, wtr_done, wt_ok, pv_done,
         ktr_done, kta_ok, ktd_ok, sqk_done, s_nmax, s_probs, s_comb, swt_done, swt_ok, so_done, so_sq, sss_done,
         srinv, attn_done, kv_used) = (sem(n) for n in (
            "in_rows in_x in_misc consts par_tr par_ok xt_done xt_copied lam_ok "
            "in_evac hg_pre hg_exp hg_ready gram_done gram_used kdt_done kdt_ok vm_ok u_done us_done "
            "states_ok sn_ok s0_land o_done o_sq ss_done rinv_ok hg_done hg_stored "
            "ko_done ko_ok kv_stored qp_ok qk_done nmax_ok probs_ok w_ok wtr_done wt_ok pv_done "
            "ktr_done kta_ok ktd_ok sqk_done s_nmax s_probs s_comb swt_done swt_ok so_done so_sq sss_done "
            "srinv attn_done kv_used").split())
        inv_mm, inv_dve = ([sem(f"{n}{g}") for g in range(2)]
                           for n in ("inv_mm", "inv_dve"))
        whi_ok, wlo_ok, xhi_ok, xlo_ok, hhi_ok, hlo_ok = (sem(n) for n in (
            "whi_ok", "wlo_ok", "xhi_ok", "xlo_ok", "hhi_ok", "hlo_ok"))
        passed = sem("passed")
        kv_land = [sem(f"kv_land{n}") for n in range(KV_SLOTS)]
        kv_odd_land = [sem(f"kv_odd_land{n}") for n in range(KV_SLOTS)]
        (ln_acc, ln_mean, ln_xc, ln_sq, ln_sqsum, ln_var, ln_rstd, ln_y, ln_done, relu_ok, hid_ok,
         p_land, pt_tr, pt_ok, gate_ok, ple_ct) = (sem(n) for n in (
            "ln_acc ln_mean ln_xc ln_sq ln_sqsum ln_var ln_rstd ln_y ln_done relu_ok hid_ok "
            "p_land pt_tr pt_ok gate_ok ple_ct").split())
        rkv_st = [sem(f"rkv_st{n}") for n in range(4)]
        (sg_ok, sg_tr, sg_rows, shift_stored, xm_ok, xm_used, lora_ok, rw_masks, rkv_land, lora2_land, ws_land,
         rw_mm, rw_dve, rw_act, rw_tr, rw_trc, gr_done, gr_used, akv_done, akv_ok,
         tat_done, tat_ok, rkv_used, ws_tr, ws_ok, us_mm, us_cp, st_mm, st_ok, tatm_ok, usm_ok, y_done, y_ok,
         sst_mm, sst_ok, so_tr, so_ok, wkv_stored, gn_mm, gn_dve, gn_act, rw_out, y_tr, y_rows, y_stored) = (
            sem(n) for n in (
            "sg_ok sg_tr sg_rows shift_stored xm_ok xm_used lora_ok rw_masks rkv_land lora2_land ws_land "
            "rw_mm rw_dve rw_act rw_tr rw_trc gr_done gr_used akv_done akv_ok "
            "tat_done tat_ok rkv_used ws_tr ws_ok us_mm us_cp st_mm st_ok tatm_ok usm_ok y_done y_ok "
            "sst_mm sst_ok sot_tr sot_ok wkv_stored gn_mm gn_dve gn_act rw_out y_tr y_rows y_stored").split())

        scratch = nc.dram_tensor("rkv_scratch", [3, KT, P, T], F32, kind="Internal").ap()

        def pset(q, lo=0, n=T, r0=0, r1=P):
            return ps[r0:r1, q * 3 * BANK + lo:q * 3 * BANK + lo + n]

        def quad(q, r0=0, r1=P):
            return ps[r0:r1, q * 4 * BANK:(q + 1) * 4 * BANK].rearrange("p (b c) -> p b c", c=BANK)[:, :, 0:QUAD]

        def quads(t):
            return t.rearrange("p (b c) -> p b c", c=QUAD)

        def bank(b, n=BANK, lo=0, r0=0, r1=P):
            return ps[r0:r1, b * BANK + lo:b * BANK + lo + n]

        def kv_slot(n):
            s = n % KV_SLOTS
            at = s * 1024 if s < 3 else KT * T + (s - 3) * 1024
            return (e["KV"] if s < 3 else big)[:, at:at + 1024]

        def load_pages(eng, i, odd, land):
            eng.wait_ge(hg_done, i + 1)
            eng.wait_ge(hg_stored, 32 * i + 32)
            eng.sem_inc(passed, 1)
            for n in range(2 * NSEQ):
                cache = a["cache_k"][0].rearrange("n p h c d -> n p h (c d)") if n < NSEQ else a["cache_v"][0]
                if n >= KV_SLOTS:
                    eng.wait_ge(kv_used, i * 16 + n - KV_SLOTS + 1)
                    eng.sem_inc(passed, 1)
                for g in range(odd, PAGES, 2):
                    page = eng.value_load(pages[0:1, n % NSEQ * PAGES + g:n % NSEQ * PAGES + g + 1],
                                          min_val=0, max_val=a["cache_k"].shape[1] - 1)
                    eng.dma_start(kv_slot(n)[:, g * P:(g + 1) * P],
                                  cache[bass.ds(page, 1), :, bass.ds(i, 1), :].rearrange("a p b d -> p (a b d)")
                                  ).then_inc(land[n % KV_SLOTS], 16)

        block = ctx.enter_context(nc.Block())

        @block.sync
        def _(sp):
            rows0 = [(a[n], 16) for n in ("ln1_g", "ln1_b", "ln2_g", "ln2_b")] + [(a["rw_mix"], 48)]
            rows1 = [(a["state_shift"], 64)] + [(a[n], 8) for n in (
                "rw_w0", "rw_a0", "rw_k_k", "rw_k_a", "rw_lnx_g", "rw_lnx_b", "rw_r_k")] + [
                (a["hg_norm_g"], 1), (a["da_norm_g"], 1), (a["hg_lb_logits"], 4)]
            for half, rows in ((0, rows0), (1, rows1)):
                at = 0
                for src, n in rows:
                    flat = src.flatten().rearrange("(r c) -> r c", c=P)
                    sp.dma_start(prow[at:at + n, half * P:(half + 1) * P], flat).then_inc(in_rows, 16)
                    at += n
            sp.dma_start(pages[0:1, :], a["page_table"].flatten().rearrange("(a n) -> a n", a=1)).then_inc(in_misc, 16)
            for n, name in enumerate(("da_lam_q1", "da_lam_k1", "da_lam_q2", "da_lam_k2")):
                sp.dma_start(lamv[:, n * 64:(n + 1) * 64], a[name].broadcast_to([P, 64])).then_inc(in_misc, 16)
            sp.dma_start(xin[:, 0:BLKS * D].rearrange("p (n c) -> p n c", c=D),
                         a["x_prompt"][0].rearrange("(n p) c -> p n c", p=P)).then_inc(in_x, 16)
            sp.dma_start(xin[0:TS, BLKS * D:9 * D], a["x_sample"].rearrange("b t c -> (b t) c")).then_inc(in_x, 16)

            def load_unit(stage, i, u, src, kt=KT, width=P):
                slot, used = unit(stage, i, u)
                sp.wait_ge(w_used[slot], used + 1)
                dst = ring[:, slot * 1024:slot * 1024 + kt * width].rearrange("p (k c) -> p k c", c=width)
                sp.dma_start(dst, src.rearrange("(k p) c -> p k c", p=P)).then_inc(w_land[slot], 16)

            def load_in(i, jobs):
                for j in jobs:
                    part = (0, 1, 3, 2, 4, 5, 6)[j]
                    load_unit("in", i, j, a["w_in_even"][0][:, bass.ds(i * P + part * 512, P)])

            def load_s0(i):
                if not isinstance(i, int) or i:
                    sp.wait_ge(attn_done, i)
                sp.dma_start(e["S0"].rearrange("p (b v) -> p b v", v=P),
                             a["state_hgrn"][0][:, bass.ds(i, 1)].rearrange("b a k v -> k (a b) v")
                             ).then_inc(s0_land, 16)

            def load_kv(i):
                load_pages(sp, i, 0, kv_land)

            sp.wait_ge(in_misc, 5 * 16)
            load_in(0, range(7))
            load_s0(0)
            with sp.Fori(0, HEADS - 1) as i:
                load_in(i + 1, range(SLOTS))
                load_kv(i)
                load_s0(i + 1)
                load_in(i + 1, range(SLOTS, 7))
            load_kv(HEADS - 1)

            def load_square(stage, src):
                with sp.Fori(0, STAGES[stage][0]) as i:
                    for j in range(4):
                        load_unit(stage, i, j, src[:, bass.ds(i * 512 + j * P, P)])

            def load_mlp(layer):
                with sp.Fori(0, 4) as i:
                    for j in range(KT):
                        load_unit(f"mlp{layer}", i, j, a["mlp_up"][layer][:, bass.ds(i * 1024 + j * P, P)])
                    for j in range(KT):
                        load_unit(f"mlp{layer}", i, KT + j,
                                  a["mlp_down"][layer][bass.ds(i * 1024, 1024), j * P:(j + 1) * P])
                sp.wait_ge(ln_acc, 2 * layer + 2)
                sp.dma_start(pl["ROWS"][:, 0:BLKS * PLE].rearrange("p (n c) -> p n c", c=PLE),
                             a["p_prompt"][layer, 0].rearrange("(n p) c -> p n c", p=P)).then_inc(p_land, 16)
                sp.dma_start(pl["ROWS"][0:TS, BLKS * PLE:9 * PLE],
                             a["p_sample"][layer].rearrange("b t c -> (b t) c")).then_inc(p_land, 16)
                with sp.Fori(0, 4) as i:
                    for j in range(2):
                        cols = bass.ds(i * 256 + j * P, P)
                        load_unit(f"ple{layer}", i, 2 * j, a["ple_gate"][layer][:, cols])
                        load_unit(f"ple{layer}", i, 2 * j + 1, a["ple_proj"][layer][:, cols], kt=2)

            load_square("out", a["w_out_even"][0])
            load_mlp(0)
            load_unit("lora", 0, 0, a["rw_w1"][0], width=64)
            load_unit("lora", 0, 1, a["rw_a1"][0], width=64)
            load_unit("lora", 0, 2, a["rw_g1"][0][:, 0:P])
            load_unit("lora", 0, 3, a["rw_g1"][0][:, P:160], width=32)
            for name in "rkv":
                load_square(name, a["rw_w_" + name][0])

            def load_core(i, first=False):
                cols = bass.ds(i * P, P)
                for n, name in enumerate("RKV"):
                    sp.dma_start(w[name], scratch[n, bass.ds(i, 1)].rearrange("a p t -> p (a t)")).then_inc(rkv_land, 16)
                sp.dma_start(lora2[0:64, 0:P], a["rw_w2"][0][:, cols]).then_inc(lora2_land, 16)
                sp.dma_start(lora2[64:P, 0:P], a["rw_a2"][0][:, cols]).then_inc(lora2_land, 16)
                sp.dma_start(lora2[:, P:2 * P], a["rw_g2"][0][0:P, cols]).then_inc(lora2_land, 16)
                sp.dma_start(lora2[0:32, 2 * P:3 * P], a["rw_g2"][0][P:160, cols]).then_inc(lora2_land, 16)
                if not first:
                    sp.wait_ge(ws_tr, i)
                for h in range(2):
                    src = a["state_wkv"][0][:, bass.ds(i * 2 + h, 1)].rearrange("b a v k -> v (a b) k")
                    dst = w["WS"].rearrange("p (b c) -> p b c", c=P)[h * 64:(h + 1) * 64, :, h * 64:(h + 1) * 64]
                    sp.dma_start(dst, src).then_inc(ws_land, 16)

            for n in range(4):
                sp.wait_ge(rkv_st[n], 16 + 16 * 6)
            sp.wait_ge(xm_used, 6)
            sp.wait_ge(rw_masks, 1)
            load_core(0, True)
            with sp.Fori(1, KT) as i:
                sp.wait_ge(rkv_used, i)
                load_core(i)
            sp.wait_ge(rw_out, KT)
            load_square("rout", a["rw_w_o"][0])
            load_mlp(1)
            for b in range(9):
                n = P if b < BLKS else TS
                dst = o["y_prompt"][0][b * P:(b + 1) * P, :] if b < BLKS else \
                    o["y_sample"].rearrange("b t c -> (b t) c")
                sp.wait_ge(y_rows, b + 1)
                sp.dma_start(dst, yout[0:n, b * D:(b + 1) * D]).then_inc(y_stored, 16)
            sp.wait_ge(y_stored, 9 * 16)
            sp.wait_ge(shift_stored, 2 * 16)
            sp.wait_ge(kv_stored, HEADS * 4 * 16)
            sp.wait_ge(hg_stored, HEADS * 2 * 16)
            sp.wait_ge(wkv_stored, KT * 4 * 16)

        @block.gpsimd
        def _(pool):
            def fill(t, value):
                pool.drain()
                pool.memset(t, value)

            def keep(t, pattern, base, cm, fill=0.0):
                pool.drain()
                pool.affine_select(out=t, in_=t, compare_op=ALU.is_ge, fill=fill, base=base,
                                   pattern=pattern, channel_multiplier=cm)

            def eye(t, n=P):
                fill(t, 1.0)
                keep(t, [[-1, n]], 0, 1)
                keep(t, [[1, n]], 0, -1)

            eye(ident[:, :])
            fill(ones[:, :], 1.0)
            fill(headones[:, :], 0.0)
            pool.drain()
            fill(headones[0:64, 0:64], 1.0)
            fill(headones[64:P, 64:P], 1.0)
            eye(ist[0:64, :], 64)
            eye(ist[64:P, :], 64)
            fill(causal[:, :], 0.0)
            keep(causal[:, :], [[-1, P]], 0, 1, NEG)
            fill(newmask[:, :], 0.0)
            for r in (0, 64):
                nm = newmask[r:r + 64, :]
                keep(nm, [[-1, 64]], 0, 1, NEG)
                keep(nm, [[8, 8], [0, 8]], 7, -1, NEG)
            for col, v in ((EPS_LN, 1e-5), (EPS_RMS, 1e-6), (EPS_GN, 64e-5), (TEN_LN2, 10 * math.log(2.0))):
                fill(col, v)
            fill(bmask, 1.0)
            keep(bmask, [[-8, 8]], 0, 1)
            keep(bmask, [[8, 8]], 7, -1)
            fill(qa[:, :], 0.0)
            fill(reset[:, :], 1.0)
            fill(e["RM"], 1.0)
            pool.drain()
            fill(reset[:, 0:TP:CH], 0.0)
            fill(reset[:, TP:T:LSEQ], 0.0)
            fill(e["RM"][:, 0:TP:P], 0.0)
            fill(e["RM"][:, TP:T:LSEQ], 0.0)
            eye(e["MK"][:, 0:P])
            for lv in range(1, LEVELS + 1):
                m = 1 << (lv - 1)
                mk = e["MK"][:, lv * P:(lv + 1) * P]
                fill(mk, 0.0)
                pool.drain()
                up = mk.rearrange("p (n h m) -> p n h m", h=2, m=m)[:, :, 1, :]
                fill(up, 1.0)
                keep(up, [[-2 * m, P // (2 * m)], [0, m]], 0, 1)
                keep(up, [[2 * m, P // (2 * m)], [0, m]], m - 1, -1)
            pool.drain().then_inc(consts, 1)

            pool.wait_ge(in_misc, 5 * 16)
            with pool.Fori(0, HEADS) as i:
                pool.wait_ge(states_ok, i + 1)
                pool.wait_ge(sn_ok, i + 1)
                pool.dma_start(o["hgrn_prompt"][0, 0, bass.ds(i, 1)].rearrange("a k v -> k (a v)"),
                               e["SS"][:, 8 * P:9 * P]).then_inc(hg_stored, 16)
                pool.dma_start(o["hgrn_sample"][0][:, bass.ds(i, 1)].rearrange("b a k v -> k (a b) v"),
                               e["SN"].rearrange("p (b v) -> p b v", v=P)).then_inc(hg_stored, 16)
                pool.wait_ge(ko_ok, i + 1)
                for name, t in (("k", e["KO"]), ("v", e["DV"])):
                    dp = o[name + "_prompt"][0, 0].flatten().rearrange("(n p c) -> p n c", p=P, c=512)
                    ds_ = o[name + "_sample"][0].flatten().rearrange("(r c) -> r c", c=512)
                    pool.dma_start(dp[:, :, bass.ds(i * P, P)], blocks(t)).then_inc(kv_stored, 16)
                    pool.dma_start(ds_[:, bass.ds(i * P, P)], t[0:TS, 1024:1152]).then_inc(kv_stored, 16)
                load_pages(pool, i, 1, kv_odd_land)

            def norm_sums(n):
                for k in range(1, KT, 2):
                    pool.wait_ge(ln_sq, 8 * n + k + 1)
                    pool.tensor_tensor(ln[f"SQ{k}"], ln[f"SQ{k}"], ln[f"SQ{k - 1}"], ALU.add)
                    pool.drain().then_inc(ln_sqsum, 1)

            norm_sums(0)
            norm_sums(1)
            pool.wait_ge(ple_ct, 2 + KT)
            g3 = gmask.rearrange("p (r t) -> p r t", r=2)
            fill(gmask, 1.0)
            keep(g3, [[1, 2], [1, P]], -1, -1)
            pool.drain()
            fill(g3[0:64, :, 64:P], 0.0)
            s4 = smask.rearrange("p (r b t) -> p r b t", r=2, b=8)
            fill(smask, 1.0)
            keep(smask.rearrange("p (r t) -> p r t", r=2), [[1, 2], [1, 64]], -1, -1)
            keep(s4, [[0, 2], [-8, 8], [0, 8]], 0, 1)
            keep(s4, [[0, 2], [8, 8], [0, 8]], 7, -1)
            fill(lmask, 0.0)
            for lv in range(RWL):
                m = 1 << lv
                pool.drain()
                for r in (0, 64):
                    v = lmask[r:r + 64, lv * CH:(lv + 1) * CH].rearrange("p (n h m) -> p n h m", h=2, m=m)[:, :, 0, :]
                    fill(v, 1.0)
                    keep(v, [[-2 * m, CH // (2 * m)], [0, m]], -m, 1)
                    keep(v, [[2 * m, CH // (2 * m)], [0, m]], 2 * m - 1, -1)
            fill(umask, 0.0)
            for r in (0, 64):
                v = umask[r:r + 64, :].rearrange("p (n h) -> p n h", h=2)[:, :, 1]
                fill(v, 1.0)
                keep(v, [[-2, CH // 2]], 0, 1)
                keep(v, [[2, CH // 2]], 0, -1)
            for n in range(4):
                pool.wait_ge(rkv_st[n], 16 + 16 * 6)
            fill(w["WS"], 0.0)
            pool.drain().then_inc(rw_masks, 1)
            with pool.Fori(0, KT) as i:
                pool.wait_ge(so_ok, i + 1)
                so = w["SO"].rearrange("p (b c) -> p b c", c=P)
                for h in range(2):
                    rows, cols = slice(h * 64, h * 64 + 64), slice(h * 64, h * 64 + 64)
                    pool.dma_start(o["wkv_sample"][0][:, bass.ds(i * 2 + h, 1)].rearrange("b a v k -> v (a b) k"),
                                   so[rows, 0:8, cols]).then_inc(wkv_stored, 16)
                    pool.dma_start(o["wkv_prompt"][0, 0, bass.ds(i * 2 + h, 1)].rearrange("a v k -> v (a k)"),
                                   so[rows, 8, cols]).then_inc(wkv_stored, 16)
            norm_sums(2)
            norm_sums(3)

        @block.scalar
        def _(act):
            def f(out, in_, func, **kw):
                return act.activation(out, in_, func, **kw)

            for q in range(2):
                act.drain().then_inc(job_free[q], 1)
            for n in range(4):
                act.drain().then_inc(rkv_st[n], 16)
            act.wait_ge(par_tr, 1)
            f(par[:, 0:112], bank(6, 112), ACT.Copy)
            f(par[:, P:P + 126], bank(6, 126, P), ACT.Copy)
            act.drain().then_inc(par_ok, 1)
            for k in range(KT):
                act.wait_ge(xt_done, k + 1)
                f(xs(xa, k), pset(k % 2), ACT.Copy).then_inc(xt_copied, 1)

            def rsqrt_mean(dst, src, n, eps):
                f(dst, src, ACT.Ln, scale=1.0 / n, bias=eps)
                act.drain()
                return f(dst, dst, ACT.Exp, scale=-0.5)

            def by_block(dst, q):
                f(dst[:, 0:1024], pset(q, 0, 1024), ACT.Copy)
                return f(dst[0:TS, 1024:1152], pset(q, 1024, P, 0, TS), ACT.Copy)

            act.wait_ge(lam_ok, 1)
            f(small[:, 20:22], small[:, 18:20], ACT.Exp)
            f(small[:, 12:16], small[:, 8:12], ACT.Exp)
            act.drain().then_inc(lam_ok, 1)

            with act.Fori(0, HEADS) as i:
                def job_is_done(j):
                    q, used, n = job("in", i, j)
                    act.wait_ge(job_done, n + 1)
                    return q

                q = job_is_done(0)
                f(e["T1"], pset(q), ACT.Sigmoid).then_inc(in_evac, 1)
                q = job_is_done(1)
                f(e["FH"], pset(q), ACT.Sigmoid).then_inc(job_free[q], 1)
                act.drain().then_inc(in_evac, 1)
                q = job_is_done(2)
                f(e["HG"], pset(q), ACT.Sigmoid).then_inc(job_free[q], 1)
                act.drain().then_inc(in_evac, 1)
                act.wait_ge(hg_pre, i * 10 + 1)
                f(e["T1"], e["T1"], ACT.Ln)
                f(e["EB"], e["EB"], ACT.Ln)
                act.drain().then_inc(hg_exp, 1)
                q = job_is_done(3)
                by_block(e["VH"], q).then_inc(job_free[q], 1)
                act.drain().then_inc(in_evac, 1)
                act.wait_ge(hg_pre, i * 10 + 2)
                f(e["EB"], e["GH"], ACT.Exp).then_inc(hg_exp, 1)
                act.wait_ge(hg_pre, i * 10 + 3)
                f(e["T1"], e["T1"], ACT.Exp).then_inc(hg_exp, 1)
                for lv in range(LEVELS):
                    act.wait_ge(hg_pre, i * 10 + 4 + lv)
                    n = T if lv < 3 else TP
                    t = e["ML"][:, lv * T:lv * T + n]
                    f(t, t, ACT.Exp).then_inc(hg_exp, 1)
                q = job_is_done(4)
                f(e["DQ"], pset(q), ACT.Copy).then_inc(job_free[q], 1)
                act.drain().then_inc(in_evac, 1)
                q = job_is_done(5)
                f(e["DK"], pset(q), ACT.Copy).then_inc(job_free[q], 1)
                act.drain().then_inc(in_evac, 1)
                q = job_is_done(6)
                by_block(e["DV"], q).then_inc(job_free[q], 1)
                act.drain().then_inc(in_evac, 1)
                act.wait_ge(kdt_done, i + 1)
                by_block(e["KDT"], 1)
                act.drain().then_inc(kdt_ok, 1)
                act.wait_ge(o_done, i + 1)
                f(e["QH"], pset(0), ACT.Square).then_inc(o_sq, 1)
                act.wait_ge(ss_done, i + 1)
                rsqrt_mean(e["T1"], pset(1), P, EPS_RMS).then_inc(rinv_ok, 1)
                act.wait_ge(ko_done, i + 1)
                by_block(e["KO"], 1)
                act.drain().then_inc(ko_ok, 1)
                act.wait_ge(hg_done, i + 1)
                act.wait_ge(hg_stored, 32 * i + 32)
                for qb in range(BLKS):
                    n = (qb + 1) * P
                    act.wait_ge(nmax_ok, i * 8 + qb + 1)
                    if qb:
                        act.wait_ge(wtr_done, i * 12 + (qb if qb < 5 else 2 * qb - 4))
                    f(e["P0"][:, 0:n], bank(3, n), ACT.Exp, scale=0.125, bias=small[:, 26:27],
                      accum_out=small[:, 28:29])
                    f(e["P1"][:, 0:n], bank(6, n), ACT.Exp, scale=0.125, bias=small[:, 27:28],
                      accum_out=small[:, 29:30])
                    act.drain().then_inc(probs_ok, 1)
                    for g in range(1 if qb < 4 else 2):
                        m = min(4, qb + 1 - 4 * g) * P
                        act.wait_ge(wtr_done, i * 12 + (qb if qb < 5 else 2 * qb - 4) + g + 1)
                        if g == 0 and qb:
                            act.wait_ge(pv_done, i * 8 + qb)
                        f(e["WT"][:, g * 512:g * 512 + m], bank(5, m), ACT.Copy)
                        act.drain().then_inc(wt_ok, 1)
                for b in range(NSEQ):
                    act.wait_ge(ktr_done, i * 16 + 2 * b + 1)
                    if b:
                        act.wait_ge(sqk_done, i * 16 + 2 * b - 1)
                    f(e["KTS"][:, 0:512], bank(6), ACT.Copy).then_inc(kta_ok, 1)
                act.wait_ge(s_nmax, i + 1)
                f(e["P0"], pset(1), ACT.Exp, scale=0.125, bias=small[:, 31:32], accum_out=small[:, 32:33])
                act.drain().then_inc(s_probs, 1)
                act.wait_ge(swt_done, i + 1)
                f(e["WTS"][:, 0:512], bank(6), ACT.Copy)
                f(e["WTS"][0:TS, 512:576], bank(7, 64, 0, 0, TS), ACT.Copy)
                act.drain().then_inc(swt_ok, 1)
                act.wait_ge(so_done, i + 1)
                f(e["P1"], pset(0), ACT.Square).then_inc(so_sq, 1)
                act.wait_ge(sss_done, i + 1)
                rsqrt_mean(e["P0"], pset(1), P, EPS_RMS).then_inc(srinv, 1)
                act.wait_ge(kv_stored, 64 * i + 64)

            def norm(n, src, dst, g, b):
                for k in range(KT):
                    act.wait_ge(ln_xc, 8 * n + k + 1)
                    f(ln[f"SQ{k}"], xs(src, k), ACT.Square).then_inc(ln_sq, 1)
                act.wait_ge(ln_var, n + 1)
                rsqrt_mean(ln["RSTD"], pset(1), D, EPS_LN).then_inc(ln_rstd, 1)
                for k in range(KT):
                    act.wait_ge(ln_y, 8 * n + k + 1)
                    f(xs(dst, k), xs(src, k), ACT.Identity, scale=par[:, g + k:g + k + 1],
                      bias=par[:, b + k:b + k + 1]).then_inc(ln_done, 1)
                    if n % 2 == 0:
                        act.drain()
                        f(xs(x_hi, k), xs(dst, k), ACT.Copy).then_inc(xhi_ok, 1)

            def mlp(layer):
                stage = f"mlp{layer}"
                with act.Fori(0, 4) as i:
                    for j in range(2 * KT):
                        slot, used = unit(stage, i, j)
                        act.wait_ge(w_land[slot], used * 16 + 16)
                        act.wait_ge(job_done, job(stage, i, j)[2] - 1)
                        f(w_hi[j % 2], ring[:, slot * 1024:(slot + 1) * 1024], ACT.Copy).then_inc(whi_ok, 1)
                        if 1 <= j <= KT:
                            t = j - 1
                            q, used, n = job(stage, i, t)
                            act.wait_ge(job_done, n + 1)
                            act.wait_ge(hlo_ok, i * 9 + (36 * layer + t + 1))
                            f(quads(hidden), quad(q), ACT.Relu).then_inc(job_free[q], 1)
                            act.drain().then_inc(relu_ok, 1)
                            act.wait_ge(hid_ok, i * 8 + (32 * layer + t + 1))
                            f(xs(h_hi, t), hidden, ACT.Copy).then_inc(hhi_ok, 1)
                norm(2 * layer + 1, xa, xa, 32 + 8 * layer, 48 + 8 * layer)
                for k in range(2):
                    act.wait_ge(pt_tr, 2 * layer + k + 1)
                    f(xs(pl["PT"], k), pset(k), ACT.Copy)
                act.drain().then_inc(pt_ok, 1)
                with act.Fori(0, 4) as i:
                    for j in range(2):
                        q, used, n = job(f"ple{layer}", i, 2 * j)
                        act.wait_ge(job_done, n + 1)
                        act.wait_ge(ple_ct, i * 2 + (8 * layer + j + 1))
                        f(quads(xs(pl["GATE"], j)), quad(q), ACT.Sigmoid).then_inc(job_free[q], 1)
                        act.drain().then_inc(gate_ok, 1)

            norm(0, xa, xa, 0, 16)
            mlp(0)
            act.wait_ge(sg_tr, 1)
            f(rows4[2][0:72, 0:P], bank(7, P, QUAD, 0, 72), ACT.Copy)
            act.drain().then_inc(sg_rows, 1)
            act.dma_start(o["shift_prompt"][0].rearrange("a (k c) -> (a k) c", c=P),
                          rows4[2][0:8, 0:P]).then_inc(shift_stored, 16)
            act.dma_start(o["shift_sample"][0].rearrange("b (k c) -> (b k) c", c=P),
                          rows4[2][8:72, 0:P]).then_inc(shift_stored, 16)
            for j, (dst, src, func) in enumerate((
                    (hid_wa[0:64, :], (0, 64), ACT.Tanh), (hid_wa[64:P, :], (64, P), ACT.Copy),
                    (hid_g1, (0, P), ACT.Sigmoid), (hid_g2[0:32, :], (0, 32), ACT.Sigmoid))):
                q, used, n = job("lora", 0, j)
                act.wait_ge(job_done, n + 1)
                f(quads(dst), quad(q, *src), func).then_inc(job_free[q], 1)
            act.drain().then_inc(lora_ok, 1)
            act.wait_ge(shift_stored, 32)
            for m, name in enumerate("rkv"):
                with act.Fori(0, 2) as i:
                    for j in range(4):
                        q, used, n = job(name, i, j)
                        act.wait_ge(job_done, n + 1)
                        act.wait_ge(rkv_st[j], 16 * i + 16 * (2 * m + 1))
                        f(quads(rows4[j]), quad(q), ACT.Copy).then_inc(job_free[q], 1)
                        act.drain().then_inc(w_used[unit(name, i, j)[0]], 1)
                        act.dma_start(scratch[m, bass.ds(i * 4 + j, 1)].rearrange("a p t -> p (a t)"),
                                      rows4[j]).then_inc(rkv_st[j], 16)

            with act.Fori(0, KT) as i:
                act.wait_ge(rw_dve, i * 6 + 1)
                act.wait_ge(rw_mm, i * 5 + 1)
                f(w["LW"], pset(0), ACT.Sigmoid, bias=cur[:, 0:1]).then_inc(rw_act, 1)
                act.wait_ge(rw_mm, i * 5 + 2)
                f(w["SA"], pset(1), ACT.Sigmoid, bias=cur[:, 1:2]).then_inc(rw_act, 1)
                act.wait_ge(rw_mm, i * 5 + 3)
                f(w["GT"], pset(0), ACT.Copy).then_inc(rw_act, 1)
                act.wait_ge(rw_dve, i * 6 + 2)
                f(w["RN"], w["KK"], ACT.Square).then_inc(rw_act, 1)
                f(w["EP"], w["C"], ACT.Exp)
                f(w["EPP"], w["EPP"], ACT.Exp)
                act.drain()
                f(w["C"], w["C"], ACT.Exp, scale=-1.0)
                act.drain().then_inc(rw_act, 1)
                act.wait_ge(rw_dve, i * 6 + 3)
                f(w["RN"], w["RN"], ACT.Ln)
                act.drain()
                f(w["RN"], w["RN"], ACT.Exp, scale=-0.5, bias=TEN_LN2).then_inc(rw_act, 1)
                for n, name in enumerate(("ATK", "BTK", "KTK", "VTK")):
                    act.wait_ge(rw_tr, i * 4 + n + 1)
                    by_block(w[name], (n + 1) % 2)
                    act.drain().then_inc(rw_trc, 1)
                for h in range(2):
                    act.wait_ge(akv_done, i * 2 + h + 1)
                    f(w["AKV"][:, h * 576:h * 576 + 512], bank(0), ACT.Copy)
                    f(w["AKV"][0:TS, h * 576 + 512:h * 576 + 576], bank(1, 64, 0, 0, TS), ACT.Copy)
                    act.drain().then_inc(akv_ok, 1)
                act.wait_ge(tat_done, i + 1)
                f(w["TAT"], pset(1), ACT.Copy).then_inc(tat_ok, 1)
                act.wait_ge(ws_tr, i + 1)
                f(w["ST0"], bank(6, 1024), ACT.Copy).then_inc(ws_ok, 1)
                for c in range(NCH + 1):
                    r, blk = (c % 2 * 64, c // 2) if c < NCH else (0, BLKS)
                    act.wait_ge(us_mm, i * 17 + c + 1)
                    f(w["US"][r:r + 64, blk * P:(blk + 1) * P], bank(3 + c % 2, P, 0, r, r + 64),
                      ACT.Copy).then_inc(us_cp, 1)
                act.wait_ge(y_done, i + 1)
                f(w["YS"], pset(0), ACT.Copy).then_inc(y_ok, 1)
                act.wait_ge(so_tr, i + 1)
                f(w["SO"], pset(1, 0, 1152), ACT.Copy)
                act.drain().then_inc(so_ok, 1)
                act.wait_ge(gn_dve, i * 2 + 1)
                f(w["SQ"], w["YS"], ACT.Square).then_inc(gn_act, 1)
                act.wait_ge(gn_mm, i * 2 + 2)
                rsqrt_mean(w["RS"], pset(0), 64, EPS_GN).then_inc(gn_act, 1)
                act.wait_ge(wkv_stored, i * 64 + 64)
            norm(2, lo8, xa, 8, 24)
            mlp(1)
            for b in range(0, 9, 2):
                n = P if b < BLKS else TS
                act.wait_ge(y_tr, b + 1)
                f(yout[0:n, b * D:(b + 1) * D], bank(b % 4 * 2, D, 0, 0, n), ACT.Copy)
                act.drain().then_inc(y_rows, 1)
                if b < BLKS:
                    act.wait_ge(y_rows, b + 2)

        @block.vector
        def _(v):
            def tt(out, x, y, op):
                return v.tensor_tensor(out, x, y, op)

            for _ in range(2):
                v.drain().then_inc(ple_ct, 1)
            v.wait_ge(in_misc, 5 * 16)
            tt(lamv[:, 0:64], lamv[:, 0:64], lamv[:, 64:128], ALU.mult)
            tt(lamv[:, 128:192], lamv[:, 128:192], lamv[:, 192:256], ALU.mult)
            v.drain()
            v.tensor_reduce(small[:, 18:19], lamv[:, 0:64], AX.X, ALU.add)
            v.tensor_reduce(small[:, 19:20], lamv[:, 128:192], AX.X, ALU.add)
            v.wait_ge(par_ok, 1)
            lb = par[:, 250:254]
            v.tensor_copy(small[:, 12:16], lb)
            v.drain()
            tt(small[:, 8:12], lb, small[:, 12:16], ALU.subtract)
            v.drain().then_inc(lam_ok, 1)
            v.wait_ge(lam_ok, 2)
            tt(small[:, 22:23], small[:, 20:21], small[:, 21:22], ALU.subtract)
            v.reciprocal(small[:, 8:12], small[:, 12:16])
            v.drain()
            v.tensor_scalar(NLAM, small[:, 22:23], LAM_INIT, -1.0, ALU.add, ALU.mult)
            tt(small[:, 12:16], small[:, 12:16], small[:, 8:12], ALU.mult)
            v.wait_ge(consts, 1)
            v.memset(LAMC, 1.0)
            v.drain()
            tt(small[:, 0:4], small[:, 12:16], small[:, 12:16], ALU.subtract)
            v.tensor_copy(cst[64:P, 5:6], cst[64:P, 4:5])
            v.drain()
            v.tensor_scalar(small[:, 4:8], small[:, 0:4], -1.0, 1.0, ALU.mult, ALU.add)
            v.drain()

            seqs = lambda t: t[:, TP:T].rearrange("p (b s) -> p b s", s=LSEQ)
            with v.Fori(0, HEADS) as i:
                v.tensor_copy(cur[:, 0:1], small[:, bass.ds(i, 1)])
                v.tensor_copy(cur[:, 1:2], small[:, bass.ds(i + 4, 1)])
                v.wait_ge(in_evac, i * 7 + 1)
                q, _, _ = job("in", 0, 0)
                tt(e["QH"], e["T1"], pset(q), ALU.mult).then_inc(job_free[q], 1)
                v.drain()
                v.wait_ge(in_evac, i * 7 + 2)
                v.tensor_scalar(e["FH"], e["FH"], cur[:, 1:2], cur[:, 0:1], ALU.mult, ALU.add)
                v.drain()
                v.tensor_scalar(e["T1"], e["FH"], 2.0 ** -50, None, ALU.max)
                v.tensor_scalar(e["EB"], e["FH"], 1e-30, 2.0 ** 50, ALU.max, ALU.mult)
                v.drain()
                v.tensor_scalar(e["EB"], e["EB"], 1.0, None, ALU.min)
                v.tensor_scalar(e["FH"], e["FH"], -1.0, 1.0, ALU.mult, ALU.add)
                v.drain().then_inc(hg_pre, 1)
                v.wait_ge(hg_exp, i * 10 + 1)
                tt(e["QB"], e["T1"], e["EB"], ALU.add)
                v.drain()
                v.tensor_tensor_scan(e["GH"], e["RM"], e["QB"], 0.0, ALU.mult, ALU.add)
                v.drain().then_inc(hg_pre, 1)
                b8 = blocks(e["GH"])
                tt(blocks(e["T1"]), b8[:, :, P - 1:P].broadcast_to([P, BLKS, P]), b8, ALU.subtract)
                tt(seqs(e["T1"]), seqs(e["GH"])[:, :, 7:8].broadcast_to([P, NSEQ, LSEQ]), seqs(e["GH"]), ALU.subtract)
                v.drain().then_inc(hg_pre, 1)

                def halves(t, lv):
                    m, n = 1 << lv, (T if lv < 3 else TP)
                    r = t[:, 0:n].rearrange("p (n h m) -> p n h m", h=2, m=m)
                    return r[:, :, 0, :], r[:, :, 1, :], m, n // (2 * m)

                for lv in range(LEVELS):
                    lo, up, m, n = halves(e["GH"], lv)
                    mlo, mup, _, _ = halves(e["ML"][:, lv * T:(lv + 1) * T], lv)
                    mid = lo[:, :, m - 1:m].broadcast_to([P, n, m])
                    tt(mup, up, mid, ALU.subtract)
                    tt(mlo, mid, lo, ALU.subtract)
                    v.drain().then_inc(hg_pre, 1)
                v.wait_ge(hg_exp, i * 10 + 2)
                tt(e["QB"], e["QH"], e["EB"], ALU.mult)
                v.wait_ge(hg_exp, i * 10 + 3)
                tt(e["T1"], e["T1"], e["FH"], ALU.mult)
                for lv in range(LEVELS):
                    v.wait_ge(hg_exp, i * 10 + 4 + lv)
                    mlo, mup, _, _ = halves(e["ML"][:, lv * T:(lv + 1) * T], lv)
                    tt(mup, mup, halves(e["QH"], lv)[1], ALU.mult)
                    tt(mlo, mlo, halves(e["FH"], lv)[0], ALU.mult)
                v.drain().then_inc(hg_ready, 1)
                for blk in range(9):
                    r, nl, t = (P, 8, P) if blk < BLKS else (TS, 4, TS)
                    v.wait_ge(gram_done, i * 9 + blk + 1)
                    g3 = bank(3 if blk % 2 else 6, nl * P, 0, 0, r).rearrange("p (l t) -> p l t", t=P)[:, :, 0:t]
                    m3 = e["MK"][0:r, 0:nl * P].rearrange("p (l t) -> p l t", t=P)[:, :, 0:t]
                    gm = e["GM"][0:r, 0:nl * P].rearrange("p (l t) -> p l t", t=P)[:, :, 0:t]
                    tt(gm, g3, m3, ALU.mult)
                    v.drain().then_inc(gram_used, 1)
                    v.tensor_reduce(e["SC"][0:r, blk * P:blk * P + t], gm.rearrange("p l t -> p t l"), AX.X, ALU.add)
                    v.drain()
                tt(e["VM"][0:TS, :].rearrange("p (b c) -> p b c", c=P),
                   e["VH"][0:TS, 1024:1152].unsqueeze(1).broadcast_to([TS, NSEQ, P]),
                   bmask.unsqueeze(2).broadcast_to([TS, NSEQ, P]), ALU.mult)
                v.drain().then_inc(vm_ok, 1)
                v.wait_ge(u_done, i + 1)
                ss = lambda c: e["SS"][:, c * P:(c + 1) * P]
                v.tensor_copy(ss(1), bank(6, P))
                for c in range(1, BLKS):
                    v.drain()
                    v.scalar_tensor_tensor(out=ss(c + 1), in0=ss(c), scalar=e["EB"][:, c * P + P - 1:c * P + P],
                                           in1=bank(6, P, c * P), op0=ALU.mult, op1=ALU.add)
                v.drain().then_inc(states_ok, 1)
                v.wait_ge(s0_land, 16 * i + 16)
                v.wait_ge(us_done, i + 1)
                for b in range(NSEQ):
                    at = TP + b * LSEQ + LSEQ - 1
                    v.scalar_tensor_tensor(out=e["SN"][:, b * P:(b + 1) * P], in0=e["S0"][:, b * P:(b + 1) * P],
                                           scalar=e["EB"][:, at:at + 1], in1=bank(3, P, b * P),
                                           op0=ALU.mult, op1=ALU.add)
                v.drain().then_inc(sn_ok, 1)
                v.wait_ge(rinv_ok, i + 1)
                tt(e["QH"], pset(0), e["T1"], ALU.mult)
                v.drain()
                v.scalar_tensor_tensor(out=lo8[:, bass.ds(i * T, T)], in0=e["QH"], scalar=par[:, 248:249],
                                       in1=e["HG"], op0=ALU.mult, op1=ALU.mult)
                v.drain().then_inc(hg_done, 1)
                v.wait_ge(hg_stored, 32 * i + 32)
                v.memset(e["QP"], 0.0)
                v.drain()
                qp = e["QP"].rearrange("p (b j) -> p b j", j=136)
                for c in range(2):
                    rows = slice(64 * c, 64 * c + 64)
                    v.tensor_copy(qp[rows, :, 64 * c:64 * c + 8], seqs(e["DQ"])[rows])
                    v.tensor_copy(qa[rows, 64 * c:64 * c + 64], e["DQ"][rows, TP:T])
                v.drain().then_inc(qp_ok, 1)
                for qb in range(BLKS):
                    n = (qb + 1) * P
                    v.wait_ge(qk_done, i * 8 + qb + 1)
                    for bk in (3, 6):
                        d = bank(bk, P, qb * P)
                        tt(d, d, causal[:, :], ALU.add)
                    v.drain()
                    v.tensor_reduce(small[:, 24:25], bank(3, n), AX.X, ALU.max)
                    v.tensor_reduce(small[:, 25:26], bank(6, n), AX.X, ALU.max)
                    v.drain()
                    v.tensor_scalar(small[:, 26:28], small[:, 24:26], -0.125, None, ALU.mult)
                    v.drain().then_inc(nmax_ok, 1)
                    v.wait_ge(probs_ok, i * 8 + qb + 1)
                    v.reciprocal(small[:, 34:36], small[:, 28:30])
                    v.drain()
                    tt(small[:, 35:36], small[:, 35:36], NLAM, ALU.mult)
                    v.drain()
                    v.tensor_scalar(e["P1"][:, 0:n], e["P1"][:, 0:n], small[:, 35:36], None, ALU.mult)
                    v.drain()
                    v.scalar_tensor_tensor(out=e["P1"][:, 0:n], in0=e["P0"][:, 0:n], scalar=small[:, 34:35],
                                           in1=e["P1"][:, 0:n], op0=ALU.mult, op1=ALU.add)
                    v.drain().then_inc(w_ok, 1)
                for b in range(NSEQ):
                    v.wait_ge(ktr_done, i * 16 + 2 * b + 2)
                    if b:
                        v.wait_ge(sqk_done, i * 16 + 2 * b)
                    v.tensor_copy(e["KTS"][:, 512:1024], bank(7)).then_inc(ktd_ok, 1)
                v.wait_ge(sqk_done, i * 16 + 16)
                tt(bank(5, 64), bank(5, 64), newmask[:, :], ALU.add)
                v.drain()
                v.tensor_reduce(small[:, 30:31], pset(1), AX.X, ALU.max)
                v.drain()
                v.tensor_scalar(small[:, 31:32], small[:, 30:31], -0.125, None, ALU.mult)
                v.drain().then_inc(s_nmax, 1)
                v.wait_ge(s_probs, i + 1)
                v.reciprocal(small[:, 33:34], small[:, 32:33])
                v.drain()
                tt(small[:, 33:34], small[:, 33:34], LAMC, ALU.mult)
                v.drain()
                v.tensor_scalar(qa[:, 0:64], ist[:, :], small[:, 33:34], None, ALU.mult)
                v.drain().then_inc(s_comb, 1)
                v.wait_ge(srinv, i + 1)
                tt(e["P1"], pset(0), e["P0"], ALU.mult)
                v.drain()
                v.tensor_scalar(lo8[:, bass.ds(i * T + 4 * T, T)], e["P1"], par[:, 249:250], 1.0 - LAM_INIT,
                                ALU.mult, ALU.mult)
                v.memset(qa[:, 0:64], 0.0)
                v.drain().then_inc(attn_done, 1)

            def residual(stage, res):
                v.memset(accum[:, 0:T], 0.0)
                trips, jobs, _ = STAGES[stage]
                with v.Fori(0, trips) as i:
                    for j in range(jobs):
                        q, used, n = job(stage, i, j)
                        z = res[:, bass.ds(i * jobs * T + j * T, T)]
                        v.wait_ge(job_done, n + 1)
                        v.scalar_tensor_tensor(out=quads(z), in0=quads(z), scalar=ALPHA, in1=quad(q), op0=ALU.mult,
                                               op1=ALU.add).then_inc(job_free[q], 1)
                        v.drain().then_inc(w_used[unit(stage, i, j)[0]], 1)
                        tt(accum[:, 0:T], accum[:, 0:T], z, ALU.add)
                v.drain().then_inc(ln_acc, 1)

            def norm(n, src):
                v.wait_ge(ln_mean, n + 1)
                for k in range(KT):
                    v.scalar_tensor_tensor(out=xs(src, k), in0=pset(0), scalar=-1.0 / D, in1=xs(src, k),
                                           op0=ALU.mult, op1=ALU.add).then_inc(ln_xc, 1)
                v.drain()
                v.wait_ge(ln_rstd, n + 1)
                def low(k):
                    v.wait_ge(xhi_ok, 4 * n + k + 1)
                    tt(xs(x_lo, k), xs(xa, k), xs(x_hi, k).bitcast(F32), ALU.subtract).then_inc(xlo_ok, 1)

                for k in range(KT):
                    tt(xs(src, k), xs(src, k), ln["RSTD"], ALU.mult).then_inc(ln_y, 1)
                    if n % 2 == 0 and k >= 3:
                        low(k - 3)
                for k in range(KT - 3 if n % 2 == 0 else KT, KT):
                    low(k)

            def mlp(layer):
                stage = f"mlp{layer}"
                v.memset(z_scale, ALPHA)
                with v.Fori(0, 4) as i:
                    v.drain().then_inc(hlo_ok, 1)
                    for j in range(2 * KT + 1):
                        if j < 2 * KT:
                            slot, used = unit(stage, i, j)
                            v.wait_ge(whi_ok, i * 16 + (64 * layer + j + 1))
                            tt(w_lo[j % 2], ring[:, slot * 1024:(slot + 1) * 1024], w_hi[j % 2].bitcast(F32),
                               ALU.subtract).then_inc(w_used[slot], 1)
                            v.drain().then_inc(wlo_ok, 1)
                        t = j - 1
                        if 0 <= t < KT:
                            v.wait_ge(relu_ok, i * 8 + (32 * layer + t + 1))
                            tt(hidden, hidden, hidden, ALU.mult)
                            v.drain().then_inc(hid_ok, 1)
                            v.wait_ge(hhi_ok, i * 8 + (32 * layer + t + 1))
                            tt(xs(h_lo, t), hidden, xs(h_hi, t).bitcast(F32), ALU.subtract)
                            v.drain().then_inc(hlo_ok, 1)
                        if t == KT - 1:
                            v.memset(accum[:, 0:T], 0.0)
                            v.drain()
                        if t >= KT:
                            q, used, n = job(stage, i, t)
                            z = xs(xa, t - KT)
                            v.wait_ge(job_done, n + 1)
                            v.scalar_tensor_tensor(out=quads(z), in0=quads(z), scalar=z_scale, in1=quad(q),
                                                   op0=ALU.mult, op1=ALU.add).then_inc(job_free[q], 1)
                            v.drain()
                            tt(accum[:, 0:T], accum[:, 0:T], z, ALU.add)
                            v.drain()
                    v.memset(z_scale, 1.0)
                v.drain().then_inc(ln_acc, 1)
                norm(2 * layer + 1, xa)
                with v.Fori(0, 4) as i:
                    for j in range(2):
                        q, used, n = job(f"ple{layer}", i, 2 * j + 1)
                        v.drain()
                        v.wait_ge(gate_ok, i * 2 + (8 * layer + j + 1))
                        v.wait_ge(job_done, n + 1)
                        tt(quads(pl["TMP"]), quads(xs(pl["GATE"], j)), quad(q), ALU.mult).then_inc(job_free[q], 1)
                        v.drain()
                        tt(lo8[:, bass.ds(i * 2 * T + j * T, T)], xa[:, bass.ds(i * 2 * T + j * T, T)],
                           pl["TMP"], ALU.add).then_inc(ple_ct, 1)
                v.drain()

            residual("out", xa)
            norm(0, xa)
            mlp(0)
            last = rows4[3][:, 0:72]
            x3 = lo8.rearrange("p (k t) -> p k t", t=T)
            x4 = x3[:, :, TP:T].rearrange("p k (b s) -> p k b s", s=LSEQ)
            d3 = xa[:, :].rearrange("p (k t) -> p k t", t=T)
            d4 = d3[:, :, TP:T].rearrange("p k (b s) -> p k b s", s=LSEQ)
            v.tensor_copy(last[:, 0:8].unsqueeze(2), x3[:, :, TP - 1:TP])
            v.tensor_copy(last[:, 8:72].rearrange("p (b k) -> p k b", k=8), x4[:, :, :, 7])
            v.drain().then_inc(sg_ok, 1)
            tt(d3[:, :, 1:TP], x3[:, :, 0:TP - 1], x3[:, :, 1:TP], ALU.subtract)
            v.tensor_scalar(d3[:, :, 0:1], x3[:, :, 0:1], -1.0, None, ALU.mult)
            tt(d4[:, :, :, 1:8], x4[:, :, :, 0:7], x4[:, :, :, 1:8], ALU.subtract)
            tt(d4[:, :, :, 0], par[:, P:P + 64].rearrange("p (b k) -> p k b", k=8), x4[:, :, :, 0], ALU.subtract)
            v.drain()
            for n, m in enumerate((1, 4, 5, 0, 2, 3)):
                if n >= 2:
                    v.wait_ge(xm_used, n - 1)
                for k in range(KT):
                    at = 64 + m * 8 + k
                    v.scalar_tensor_tensor(out=xs(mixed[n % 2], k), in0=xs(xa, k), scalar=par[:, at:at + 1],
                                           in1=xs(lo8, k), op0=ALU.mult, op1=ALU.add)
                v.drain().then_inc(xm_ok, 1)

            with v.Fori(0, KT) as i:
                par7 = par[:, 192:248].rearrange("p (n k) -> p n k", k=8)
                v.tensor_copy(cur[:, 0:7].unsqueeze(2), par7[:, :, bass.ds(i, 1)])
                v.drain()
                v.tensor_scalar(cur[:, 7:8], cur[:, 3:4], -1.0, 1.0, ALU.mult, ALU.add)
                v.drain().then_inc(rw_dve, 1)
                v.wait_ge(rw_act, i * 6 + 1)
                v.tensor_scalar(w["LW"], w["LW"], -math.exp(-0.5), None, ALU.mult)
                v.drain()
                v.tensor_tensor_scan(w["C"], reset[:, :], w["LW"], 0.0, ALU.mult, ALU.add)
                v.wait_ge(rkv_land, i * 48 + 48)
                v.tensor_scalar(w["KK"], w["K"], cur[:, 2:3], None, ALU.mult)
                v.drain()
                tt(w["EPP"], w["C"], w["LW"], ALU.subtract)
                v.drain().then_inc(rw_dve, 1)
                v.wait_ge(rw_act, i * 6 + 2)
                v.tensor_scalar(w["LW"], w["SA"], cur[:, 3:4], cur[:, 7:8], ALU.mult, ALU.add)
                v.drain()
                tt(w["K"], w["K"], w["LW"], ALU.mult)
                v.wait_ge(rw_mm, i * 5 + 4)
                v.tensor_scalar(w["RN"], pset(1), 1e-24, 2.0 ** 20, ALU.max, ALU.mult)
                v.drain().then_inc(rw_dve, 1)
                v.scalar_tensor_tensor(out=w["LW"], in0=w["R"], scalar=cur[:, 6:7], in1=w["K"],
                                       op0=ALU.mult, op1=ALU.mult)
                v.drain().then_inc(rw_dve, 1)
                v.wait_ge(rw_act, i * 6 + 5)
                ar, bk = w["AR"], w["BK"]
                tt(ar[:, T:2 * T], w["R"], w["EP"], ALU.mult)
                tt(bk[:, T:2 * T], w["K"], w["C"], ALU.mult)
                v.tensor_copy(small[:, 40:56], w["EP"][:, CH - 1:TP:CH])
                v.tensor_copy(small[:, 56:64], w["EP"][:, TP + 7:T:LSEQ])
                v.wait_ge(rw_act, i * 6 + 6)
                tt(w["KK"], w["KK"], w["RN"], ALU.mult)
                v.drain()
                v.scalar_tensor_tensor(out=ar[:, 0:T], in0=w["KK"], scalar=-1.0, in1=w["EPP"],
                                       op0=ALU.mult, op1=ALU.mult)
                tt(w["SA"], w["KK"], w["SA"], ALU.mult)
                v.drain()
                tt(bk[:, 0:T], w["SA"], w["C"], ALU.mult)
                v.drain().then_inc(rw_dve, 1)
                v.wait_ge(rw_mm, i * 5 + 5)
                tt(w["BON"], pset(0), w["V"], ALU.mult)
                v.drain().then_inc(rw_dve, 1)
                g4 = gmask.rearrange("p (r t) -> p r t", r=2)
                s4 = smask.rearrange("p (r t) -> p r t", r=2)
                for h in range(2):
                    ab = w["AB"].rearrange("p (m t) -> p m t", m=2)
                    rb = w[f"RB{h}"].rearrange("p (m t) -> p m t", m=2)
                    xts = w[f"XT{h}"]
                    v.tensor_copy(blocks(w["X"]), ident[:, :].unsqueeze(1).broadcast_to([P, BLKS, P]))
                    v.tensor_copy(w["X"][0:64, TP:T], ident[0:64, 0:64])
                    if h:
                        v.wait_ge(akv_done, i * 2 + 1)
                    for blk in range(9):
                        r, t, mk = (P, P, g4) if blk < BLKS else (TS, TS, s4)
                        v.wait_ge(gr_done, i * 18 + h * 9 + blk + 1)
                        g = bank(blk % 4, BANK, 0, 0, r).rearrange("p (m r t) -> p m r t", m=2, r=2)
                        for which, dst in ((0, ab), (1, rb)):
                            last_ = tt(dst[0:r, :, blk * P:blk * P + t], g[:, :, which, 0:t],
                                       mk[:, which:which + 1, :].broadcast_to([r, 2, t]), ALU.mult)
                        v.drain().then_inc(gr_used, 1)
                    for g in range(2):
                        v.drain().then_inc(inv_dve[g], 1)
                    v3 = lambda t: t.rearrange("p (n c) -> p n c", c=CH)

                    def mask(g, lv):
                        lm = lmask[:, lv * CH:(lv + 1) * CH]
                        v.wait_ge(inv_mm[g], (i * 2 + h) * 11 + max(1, 2 * lv))
                        tt(v3(w["P1M"][:, g * 512:g * 512 + 512]), v3(bank(g)),
                           lm.unsqueeze(1).broadcast_to([P, 8, CH]), ALU.mult)
                        if g and 1 << lv < LSEQ:
                            tt(w["P1M"][0:64, TP:T], bank(2, 64, 0, 0, 64), lm[0:64], ALU.mult)
                        v.drain().then_inc(inv_dve[g], 1)

                    def grow(g, lv):
                        cols = slice(g * 512, g * 512 + 512)
                        if lv == 0:
                            parts = [(P, cols, 4, umask)] + ([(64, slice(TP, T), 1, umask[0:64])] if g else [])
                            for n, c, blks, um in parts:
                                tt(w["X"][0:n, c], w["X"][0:n, c], w["P1M"][0:n, c], ALU.add)
                                tt(xts[0:n, c].rearrange("p (n c) -> p n c", c=CH),
                                   w["AB"][0:n, c].rearrange("p (n c) -> p n c", c=CH),
                                   um.unsqueeze(1).broadcast_to([n, n * blks // CH, CH]), ALU.mult)
                                v.drain()
                                x3 = xts[0:n, c].rearrange("p (b c) -> p b c", b=blks)
                                tt(x3, x3, ident[0:n, 0:n].unsqueeze(1).broadcast_to([n, blks, n]), ALU.add)
                            v.drain().then_inc(inv_dve[g], 1)
                            return
                        v.wait_ge(inv_mm[g], (i * 2 + h) * 11 + 2 * lv + 1)
                        if lv < RWL - 1:
                            tt(w["X"][:, cols], w["X"][:, cols], bank(3 + g), ALU.add)
                        tt(xts[:, cols], xts[:, cols], bank(6 + g), ALU.add)
                        if g and 1 << lv < LSEQ:
                            tt(w["X"][0:64, TP:T], w["X"][0:64, TP:T], bank(5, 64, 0, 0, 64), ALU.add)
                            tt(xts[0:64, TP:T], xts[0:64, TP:T], bank(5, 64, 64, 0, 64), ALU.add)
                        v.drain().then_inc(inv_dve[g], 1)

                    mask(0, 0)
                    for lv in range(RWL):
                        grow(0, lv)
                        mask(1, lv)
                        if lv < RWL - 1:
                            mask(0, lv + 1)
                        grow(1, lv)
                v.memset(state[:, :], 0.0)
                v.memset(qa[:, :], 0.0)
                v.drain().then_inc(st_ok, 1)
                for c in range(NCH):
                    new, decay = (c + 1) % 2 * P, small[:, 40 + c:41 + c]
                    v.wait_ge(st_mm, i * 16 + c + 1)
                    for r in (0, 64):
                        v.scalar_tensor_tensor(out=state[r:r + 64, new + r:new + r + 64],
                                               in0=bank(6 + c % 2, 64, r, r, r + 64), scalar=decay[r:r + 64],
                                               in1=qa[r:r + 64, r:r + 64], op0=ALU.mult, op1=ALU.add)
                    v.drain().then_inc(st_ok, 1)
                    if c < NCH - 1:
                        v.tensor_scalar(qa[:, :], state[:, new:new + P], small[:, 41 + c:42 + c], None, ALU.mult)
                    v.drain()
                    if c == 0:
                        v.wait_ge(tat_ok, i + 1)
                        v.memset(w["TATM"], 0.0)
                        v.drain()
                        tm = w["TATM"].rearrange("p (b j) -> p b j", j=72)
                        v.tensor_copy(tm[:, :, 0:8], seqs(w["TAT"]))
                        tt(w["VM"][0:TS, :].rearrange("p (b c) -> p b c", c=P),
                           w["VTK"][0:TS, 1024:1152].unsqueeze(1).broadcast_to([TS, NSEQ, P]),
                           bmask.unsqueeze(2).broadcast_to([TS, NSEQ, P]), ALU.mult)
                        v.drain().then_inc(tatm_ok, 1)
                v.wait_ge(us_cp, i * 17 + 17)
                tt(w["USM"][0:TS, :].rearrange("p (b c) -> p b c", c=P),
                   w["US"][0:TS, 1024:1152].unsqueeze(1).broadcast_to([TS, NSEQ, P]),
                   bmask.unsqueeze(2).broadcast_to([TS, NSEQ, P]), ALU.mult)
                v.drain().then_inc(usm_ok, 1)
                v.wait_ge(sst_mm, i + 1)
                st3 = w["ST0"].rearrange("p (b c) -> p b c", c=P)
                tt(w["ST0"], w["ST0"], bank(6, 1024), ALU.add)
                v.drain()
                tt(st3, st3, small[:, 56:64].unsqueeze(2).broadcast_to([P, 8, P]), ALU.mult)
                v.drain()
                tt(st3, st3, headones[:, :].unsqueeze(1).broadcast_to([P, 8, P]), ALU.mult)
                v.drain().then_inc(sst_ok, 1)
                v.wait_ge(gn_mm, i * 2 + 1)
                v.scalar_tensor_tensor(out=w["YS"], in0=pset(0), scalar=-1.0 / 64, in1=w["YS"],
                                       op0=ALU.mult, op1=ALU.add)
                v.drain().then_inc(gn_dve, 1)
                v.wait_ge(gn_act, i * 2 + 2)
                tt(w["YS"], w["YS"], w["RS"], ALU.mult)
                v.drain()
                v.tensor_scalar(w["YS"], w["YS"], cur[:, 4:5], cur[:, 5:6], ALU.mult, ALU.add)
                v.drain()
                tt(w["YS"], w["YS"], w["BON"], ALU.add)
                v.drain()
                tt(xa[:, bass.ds(i * T, T)], w["YS"], w["GT"], ALU.mult)
                v.drain().then_inc(gn_dve, 1)
                v.drain().then_inc(rw_out, 1)
            residual("rout", lo8)
            norm(2, lo8)
            mlp(1)
            for b in range(1, 9, 2):
                v.wait_ge(y_tr, b + 1)
                v.wait_ge(y_rows, b)
                v.tensor_copy(yout[:, b * D:(b + 1) * D], bank(b % 4 * 2, D))
                v.drain().then_inc(y_rows, 1)

        @block.tensor
        def _(pe):
            def mm(out, lhsT, rhs, start=True, stop=True):
                return pe.matmul(out, lhsT, rhs, start=start, stop=stop, skip_group_check=True)

            def warm(b, n):
                for _ in range(n):
                    mm(bank(b, P), ones[:, :], ident[:, :])

            for s in range(SLOTS):
                pe.drain().then_inc(w_used[s], 1)
            pe.wait_ge(consts, 1)
            pe.wait_ge(in_rows, 16 * 16)
            pe.transpose(bank(6, 112), prow[0:112, 0:P], ident[0:112, 0:112])
            pe.transpose(bank(6, 126, P), prow[0:126, P:2 * P], ident[0:126, 0:126]).then_inc(par_tr, 1)
            pe.wait_ge(in_x, 32)
            for k in range(KT):
                if k >= 2:
                    pe.wait_ge(xt_copied, k - 1)
                for b in range(9):
                    n = P if b < BLKS else TS
                    last = pe.transpose(pset(k % 2, b * P, n), xin[0:n, b * D + k * P:b * D + (k + 1) * P],
                                        ident[0:n, 0:n])
                last.then_inc(xt_done, 1)
            pe.wait_ge(xt_copied, KT)

            def project(stage, i, j, units, rhs, kts=KT, m=P, row=0, width=P, release=True):
                q, used, _ = job(stage, i, j)
                pe.wait_ge(job_free[q], used + 1)
                spans = [(pset(q, lo, n), lo, n) for lo, n in SPANS] if stage == "in" else [
                    (quad(q, row, row + m)[:, b, :], b * QUAD, QUAD) for b in range(4)]
                n_units = len(units)
                for g, u in enumerate(units):
                    slot, before_ = unit(stage, i, u)
                    pe.wait_ge(w_land[slot], before_ * 16 + 16)
                    for k in range(kts):
                        for out, lo, n in spans:
                            last = mm(out, ring[:, slot * 1024 + k * width:slot * 1024 + k * width + m],
                                      xs(rhs, g * KT + k, lo, n), g == 0 and k == 0,
                                      g == n_units - 1 and k == kts - 1)
                    if release:
                        last.then_inc(w_used[slot], 1)
                (pe.drain() if release else last).then_inc(job_done, 1)

            def project_rows(stage, i, j, u, lhs):
                q, used, _ = job(stage, i, j)
                pe.wait_ge(job_free[q], used + 1)
                slot, before_ = unit(stage, i, u)
                pe.wait_ge(w_land[slot], before_ * 16 + 16)
                for b in range(9):
                    n = P if b < BLKS else TS
                    for k in range(KT):
                        last = mm(pset(q, b * P, P, 0, n), xs(lhs, k, b * P, n),
                                  ring[:, slot * 1024 + k * P:slot * 1024 + (k + 1) * P], k == 0, k == KT - 1)
                last.then_inc(w_used[slot], 1)
                pe.drain().then_inc(job_done, 1)

            def wide(q, lhsT, rhs, start=True, stop=True):
                for lo, n in SPANS:
                    last = mm(pset(q, lo, n), lhsT, rhs[:, lo:lo + n], start, stop)
                return last

            def rows_of(q, src):
                for b in range(9):
                    n = P if b < BLKS else TS
                    last = pe.transpose(pset(q, b * P, P, 0, n), src[:, b * P:b * P + n], ident[:, :])
                return last

            with pe.Fori(0, HEADS) as i:
                for j in range(7):
                    if j in (3, 6):
                        project_rows("in", i, j, j, xa)
                    else:
                        project("in", i, j, [j], xa)
                pe.wait_ge(in_evac, i * 7 + 7)
                pe.wait_ge(hg_ready, i + 1)
                ml = e["ML"]
                for blk in range(9):
                    n, nl = (P, 8) if blk < BLKS else (TS, 4)
                    bk = 3 if blk % 2 else 6
                    if blk >= 2:
                        pe.wait_ge(gram_used, i * 9 + blk - 1)
                    for lv in range(nl):
                        at = (lv - 1) * T + blk * P
                        lhsT = e["FH"][:, blk * P:blk * P + n] if lv == 0 else ml[:, at:at + n]
                        rhs = e["QH"][:, blk * P:blk * P + n] if lv == 0 else ml[:, at:at + n]
                        last = mm(bank(bk, n, lv * P, 0, n), lhsT, rhs)
                    last.then_inc(gram_done, 1)
                warm(0, 3)
                pe.wait_ge(gram_used, i * 9 + 8)
                rows_of(1, e["T1"]).then_inc(kdt_done, 1)
                pe.wait_ge(gram_used, i * 9 + 9)
                warm(0, 7)
                pe.wait_ge(kdt_ok, i + 1)
                for c in range(BLKS):
                    last = mm(bank(6, P, c * P), e["KDT"][:, c * P:(c + 1) * P], e["VH"][:, c * P:(c + 1) * P])
                last.then_inc(u_done, 1)
                pe.wait_ge(vm_ok, i + 1)
                for g in range(2):
                    last = mm(bank(3 + g), e["KDT"][0:TS, 1024:1152], e["VM"][0:TS, g * 512:(g + 1) * 512])
                last.then_inc(us_done, 1)
                warm(0, 10)
                pe.wait_ge(states_ok, i + 1)
                pe.wait_ge(s0_land, 16 * i + 16)
                for c in range(BLKS):
                    o_ = pset(0, c * P, P)
                    last = mm(o_, e["VH"][:, c * P:(c + 1) * P], e["SC"][:, c * P:(c + 1) * P], True, c == 0)
                    if c:
                        last = mm(o_, e["SS"][:, c * P:(c + 1) * P], e["QB"][:, c * P:(c + 1) * P], False, True)
                mm(pset(0, TP, TS), e["VH"][0:TS, 1024:1152], e["SC"][0:TS, TP:T], True, False)
                for b in range(NSEQ):
                    at = TP + b * LSEQ
                    last = mm(pset(0, at, LSEQ), e["S0"][:, b * P:(b + 1) * P], e["QB"][:, at:at + LSEQ],
                              False, b == NSEQ - 1)
                last.then_inc(o_done, 1)
                warm(5, 6)
                pe.wait_ge(o_sq, i + 1)
                pe.wait_ge(sn_ok, i + 1)
                wide(1, ones[:, :], e["QH"]).then_inc(ss_done, 1)
                warm(6, 16)
                pe.wait_ge(rinv_ok, i + 1)
                rows_of(1, e["DK"]).then_inc(ko_done, 1)
                warm(6, 7)
                pe.wait_ge(ko_ok, i + 1)
                pe.wait_ge(hg_done, i + 1)

                def scores(qb):
                    if qb:
                        pe.wait_ge(probs_ok, i * 8 + qb)
                    n = (qb + 1) * P
                    for c, bk in ((0, 3), (1, 6)):
                        rows = slice(64 * c, 64 * c + 64)
                        for lo in range(0, n, BANK):
                            m = min(BANK, n - lo)
                            last = mm(bank(bk, m, lo), e["DQ"][rows, qb * P:(qb + 1) * P], e["DK"][rows, lo:lo + m])
                    last.then_inc(qk_done, 1)

                scores(0)
                for qb in range(BLKS):
                    if qb + 1 < BLKS:
                        scores(qb + 1)
                    warm(2, 8 if qb == 0 else 3)
                    pe.wait_ge(w_ok, i * 8 + qb + 1)
                    done = qb if qb < 5 else 2 * qb - 4
                    for g in range(1 if qb < 4 else 2):
                        if qb or g:
                            pe.wait_ge(wt_ok, i * 12 + done + g)
                        for n in range(4 * g, min(4 * g + 4, qb + 1)):
                            last = pe.transpose(bank(5, P, (n - 4 * g) * P), e["P1"][:, n * P:(n + 1) * P], ident[:, :])
                        last.then_inc(wtr_done, 1)
                    warm(2, 2)
                    pe.wait_ge(wt_ok, i * 12 + done + (1 if qb < 4 else 2))
                    for n in range(qb + 1):
                        last = mm(pset(0, qb * P, P), e["DV"][:, n * P:(n + 1) * P], e["WT"][:, n * P:(n + 1) * P],
                                  n == 0, n == qb)
                    last.then_inc(pv_done, 1)
                pe.wait_ge(qp_ok, i + 1)

                def landed(n):
                    s = n % KV_SLOTS
                    per = len(range(s, 16, KV_SLOTS))
                    for land in (kv_land[s], kv_odd_land[s]):
                        pe.wait_ge(land, i * (64 * per) + 64 * (n // KV_SLOTS + 1))
                    return kv_slot(n)

                for b in range(NSEQ):
                    kv = landed(b)
                    for g in range(2):
                        if b:
                            pe.wait_ge(kta_ok if g == 0 else ktd_ok, i * 8 + b)
                        for n in range(4):
                            last = pe.transpose(bank(6 + g, P, n * P), kv[:, (4 * g + n) * P:(4 * g + n + 1) * P],
                                                ident[:, :])
                        last.then_inc(ktr_done, 1)
                    pe.drain().then_inc(kv_used, 1)
                    for g in range(2):
                        pe.wait_ge(kta_ok if g == 0 else ktd_ok, i * 8 + b + 1)
                        last = mm(bank(3 + g), e["QP"][:, b * P:(b + 1) * P], e["KTS"][:, g * 512:(g + 1) * 512],
                                  b == 0, b == NSEQ - 1)
                        if b == NSEQ - 1 and g == 1:
                            last = mm(bank(5, 64), qa[:, :], e["DK"][:, TP:T])
                        last.then_inc(sqk_done, 1)
                pe.wait_ge(s_comb, i + 1)
                for n in range(9):
                    m = P if n < BLKS else TS
                    last = mm(bank(6, 64, n * 64, 0, m), e["P0"][:, n * P:n * P + m], qa[:, 0:64])
                last.then_inc(swt_done, 1)
                pe.wait_ge(swt_ok, i + 1)
                mm(pset(0, TP, TS), e["DV"][0:TS, 1024:1152], e["WTS"][0:TS, 512:576], True, False)
                for b in range(NSEQ):
                    kv = landed(NSEQ + b)
                    for g in range(PAGES):
                        at = TP + b * LSEQ
                        last = mm(pset(0, at, LSEQ), kv[:, g * P:(g + 1) * P],
                                  e["WTS"][:, g * 64 + b * 8:g * 64 + b * 8 + 8], False, b == 7 and g == 7)
                    last.then_inc(kv_used, 1)
                pe.drain().then_inc(so_done, 1)
                pe.wait_ge(so_sq, i + 1)
                wide(1, ones[:, :], e["P1"]).then_inc(sss_done, 1)
                pe.wait_ge(attn_done, i + 1)

            def square(stage, rhs):
                with pe.Fori(0, 2) as i:
                    for j in range(4):
                        project(stage, i, j, [j], rhs, release=False)

            def norm(n):
                pe.wait_ge(ln_acc, n + 1)
                wide(0, ones[:, :], accum).then_inc(ln_mean, 1)
                for p in range(KT // 2):
                    pe.wait_ge(ln_sqsum, 4 * n + p + 1)
                    last = wide(1, ones[:, :], ln[f"SQ{2 * p + 1}"], p == 0, p == KT // 2 - 1)
                last.then_inc(ln_var, 1)
                if n % 2:
                    pe.wait_ge(ln_done, 8 * n + 8)

            def mlp(layer):
                with pe.Fori(0, 4) as i:
                    for j in range(2 * KT):
                        q, used, _ = job(f"mlp{layer}", i, j)
                        hi, lo = (x_hi, x_lo) if j < KT else (h_hi, h_lo)
                        pe.wait_ge(job_free[q], used + 1)
                        pe.wait_ge(wlo_ok, i * 16 + (64 * layer + j + 1))
                        for k in range(KT):
                            if j == 0:
                                pe.wait_ge(xlo_ok, 8 * layer + k + 1)
                            if j == KT and k in (0, KT - 1):
                                pe.wait_ge(hlo_ok, i * 9 + (36 * layer + (8 if k == 0 else 9)))
                            cols = slice(k * P, (k + 1) * P)
                            for n, (wt, rhs) in enumerate(((w_hi, hi), (w_hi, lo), (w_lo, hi))):
                                for b in range(4):
                                    last = mm(quad(q)[:, b, :], wt[j % 2][:, cols], xs(rhs, k, b * QUAD, QUAD),
                                              k == 0 and n == 0, k == KT - 1 and n == 2)
                        last.then_inc(job_done, 1)
                norm(2 * layer + 1)
                pe.wait_ge(p_land, 32 * layer + 32)
                for k in range(2):
                    for b in range(9):
                        n = P if b < BLKS else TS
                        last = pe.transpose(pset(k, b * P, n),
                                            pl["ROWS"][0:n, b * PLE + k * P:b * PLE + (k + 1) * P], ident[0:n, 0:n])
                    last.then_inc(pt_tr, 1)
                pe.wait_ge(pt_ok, layer + 1)
                with pe.Fori(0, 4) as i:
                    for j in range(2):
                        project(f"ple{layer}", i, 2 * j, [2 * j], xa)
                        project(f"ple{layer}", i, 2 * j + 1, [2 * j + 1], pl["PT"], kts=2)

            square("out", lo8)
            norm(0)
            mlp(0)
            pe.wait_ge(sg_ok, 1)
            pe.transpose(bank(7, P, QUAD, 0, 72), rows4[3][:, 0:72], ident[:, :]).then_inc(sg_tr, 1)
            pe.wait_ge(xm_ok, 1)
            project("lora", 0, 0, [0], mixed[0], m=64, width=64)
            pe.drain().then_inc(xm_used, 1)
            pe.wait_ge(xm_ok, 2)
            pe.wait_ge(sg_rows, 1)
            project("lora", 0, 1, [1], mixed[1], m=64, row=64, width=64)
            pe.drain().then_inc(xm_used, 1)
            pe.wait_ge(xm_ok, 3)
            project("lora", 0, 2, [2], mixed[0])
            project("lora", 0, 3, [3], mixed[0], m=32, width=32)
            pe.drain().then_inc(xm_used, 1)
            for n, name in enumerate("rkv"):
                pe.wait_ge(xm_ok, 4 + n)
                square(name, mixed[(n + 1) % 2])
                pe.drain().then_inc(xm_used, 1)

            pe.wait_ge(lora_ok, 1)
            for q, s in ((0, "v"), (1, "v")):
                used = job("rout", 0, q)[1]
                pe.wait_ge(job_free[q], used + 1)
            pe.wait_ge(rw_masks, 1)
            with pe.Fori(0, KT) as i:
                pe.wait_ge(lora2_land, i * 64 + 64)
                for lo, n in SPANS:
                    last = mm(pset(0, lo, n), lora2[0:64, 0:P], hid_wa[0:64, lo:lo + n])
                last.then_inc(rw_mm, 1)
                for lo, n in SPANS:
                    last = mm(pset(1, lo, n), lora2[64:P, 0:P], hid_wa[64:P, lo:lo + n])
                last.then_inc(rw_mm, 1)
                warm(6, 10)
                pe.wait_ge(rw_act, i * 6 + 1)
                for lo, n in SPANS:
                    mm(pset(0, lo, n), lora2[:, P:2 * P], hid_g1[:, lo:lo + n], True, False)
                    last = mm(pset(0, lo, n), lora2[0:32, 2 * P:3 * P], hid_g2[0:32, lo:lo + n], False, True)
                last.then_inc(rw_mm, 1)
                warm(6, 16)
                pe.wait_ge(rw_act, i * 6 + 4)
                wide(1, headones[:, :], w["RN"]).then_inc(rw_mm, 1)
                warm(6, 12)
                pe.wait_ge(rw_dve, i * 6 + 4)
                wide(0, headones[:, :], w["LW"]).then_inc(rw_mm, 1)
                warm(6, 22)
                pe.wait_ge(rw_dve, i * 6 + 5)
                for n, src in enumerate((w["AR"][:, 0:T], w["BK"][:, 0:T], w["BK"][:, T:2 * T], w["V"])):
                    if n == 1:
                        pe.wait_ge(rw_dve, i * 6 + 6)
                    if n >= 2:
                        pe.wait_ge(rw_trc, i * 4 + n - 1)
                    rows_of((n + 1) % 2, src).then_inc(rw_tr, 1)
                warm(6, 8)
                pe.wait_ge(rw_trc, i * 4 + 4)
                for h in range(2):
                    rows = slice(64 * h, 64 * h + 64)
                    xts = w[f"XT{h}"]
                    if h:
                        pe.wait_ge(akv_ok, i * 2 + 1)
                    arv = w["AR"].rearrange("p (m t) -> p m t", m=2)
                    for blk in range(9):
                        n = P if blk < BLKS else TS
                        at = h * 9 + blk
                        if blk >= 4:
                            pe.wait_ge(gr_used, i * 18 + at - 3)
                            if blk == BLKS:
                                pe.sem_inc(passed, 1)
                        for m in range(2):
                            g = bank(blk % 4, 256, m * 256, 0, n).rearrange("p (r t) -> p r t", r=2)[:, :, 0:n]
                            last = mm(g, w["BK"][rows, m * T + blk * P:m * T + blk * P + n],
                                      arv[rows, :, blk * P:blk * P + n])
                        last.then_inc(gr_done, 1)
                    warm(6, 6)
                    pe.wait_ge(gr_used, i * 18 + h * 9 + 9)
                    groups = ((0, 1, 2, 3), (4, 5, 6, 7, 8))

                    def place(first, blk):
                        n = P if blk < BLKS else TS
                        if blk == BLKS:
                            return {0: bank(2, n, 0, 0, n), 3: bank(5, n, 0, 0, n), 6: bank(5, n, 64, 0, n)}[first]
                        return bank(first + blk // 4, P, blk % 4 * P)

                    def tile_(t, blk):
                        n = P if blk < BLKS else TS
                        return t[0:n, blk * P:blk * P + n]

                    def part(g, lv):
                        return groups[g] if 1 << lv < LSEQ else groups[g][0:4]

                    def p1(g, lv):
                        pe.wait_ge(inv_dve[g], (i * 2 + h) * 13 + 2 * lv + 1)
                        for blk in part(g, lv):
                            last = mm(place(0, blk), tile_(w["AB"], blk), tile_(w["X"], blk))
                        last.then_inc(inv_mm[g], 1)

                    def grow(g, lv):
                        pe.wait_ge(inv_dve[g], (i * 2 + h) * 13 + 2 * lv + 2)
                        for blk in part(g, lv):
                            last = mm(place(6, blk), tile_(w["P1M"], blk), tile_(xts, blk))
                            if lv < RWL - 1:
                                last = mm(place(3, blk), tile_(xts, blk), tile_(w["P1M"], blk))
                        last.then_inc(inv_mm[g], 1)

                    p1(0, 0)
                    for lv in range(RWL):
                        if lv:
                            grow(0, lv)
                        p1(1, lv)
                        if lv == 0:
                            warm(3, 8)
                        if lv < RWL - 1:
                            p1(0, lv + 1)
                        else:
                            warm(3, 4)
                        if lv:
                            grow(1, lv)
                    for blk in range(9):
                        n = P if blk < BLKS else TS
                        last = mm(bank(0, 64, blk * 64, 0, n), w["AB"][0:n, T + blk * P:T + blk * P + n],
                                  w["VTK"][0:n, blk * P + 64 * h:blk * P + 64 * h + 64])
                    last.then_inc(akv_done, 1)
                    warm(3, 5)
                    for g in range(2):
                        pe.wait_ge(inv_dve[g], (i * 2 + h) * 13 + 13)
                pe.wait_ge(akv_ok, i * 2 + 2)
                for h in range(2):
                    for blk in range(9):
                        n = P if blk < BLKS else TS
                        last = mm(pset(1, blk * P, n, 64 * h, 64 * h + 64),
                                  w["ATK"][0:n, blk * P + 64 * h:blk * P + 64 * h + 64], tile_(w[f"XT{h}"], blk))
                last.then_inc(tat_done, 1)
                pe.drain().then_inc(rkv_used, 1)
                pe.wait_ge(ws_land, i * 32 + 32)
                for b in range(NSEQ):
                    last = pe.transpose(bank(6, P, b * P), w["WS"][:, b * P:(b + 1) * P], ident[:, :])
                last.then_inc(ws_tr, 1)
                pe.wait_ge(tat_ok, i + 1)
                pe.wait_ge(ws_ok, i + 1)

                def u_rest(c, r, blk):
                    for h in range(2):
                        last = mm(bank(3 + c % 2, 64, 64 * h, r, r + 64),
                                  w[f"XT{h}"][r:r + 64, blk * P + r:blk * P + r + 64],
                                  w["AKV"][r:r + 64, h * 576 + blk * 64:h * 576 + blk * 64 + 64], h == 0, False)
                    return last

                def y_part(rows, m, r, blk, lo, stop):
                    for h in range(2):
                        out = pset(0, lo, 64, 64 * h, 64 * h + 64)
                        tc = m * T + blk * P + r
                        last = mm(out, rows[r:r + 64, blk * P + 64 * h:blk * P + 64 * h + 64],
                                  w[f"RB{h}"][r:r + 64, tc:tc + 64], False, stop and h == 1)
                    return last

                def keys_values(c):
                    r, blk = c % 2 * 64, c // 2
                    mm(bank(6 + c % 2, P), w["KTK"][r:r + 64, blk * P:(blk + 1) * P],
                       w["VTK"][r:r + 64, blk * P:(blk + 1) * P], True, False)

                pe.sem_inc(passed, 1)
                u_rest(0, 0, 0)
                keys_values(0)
                for c in range(NCH):
                    r, blk = c % 2 * 64, c // 2
                    st = state[:, c % 2 * P:(c % 2 + 1) * P]
                    pe.wait_ge(st_ok, i * 17 + c + 1)
                    mm(bank(3 + c % 2, P, 0, r, r + 64), w["TAT"][:, c * CH:(c + 1) * CH], st,
                       False, True).then_inc(us_mm, 1)
                    mm(pset(0, c * CH, CH), st, w["AR"][:, T + c * CH:T + (c + 1) * CH], True, False)
                    if c < NCH - 1:
                        u_rest(c + 1, 64 - r, (c + 1) // 2)
                    pe.wait_ge(us_cp, i * 17 + c + 1)
                    mm(bank(6 + c % 2, P), w["BTK"][r:r + 64, blk * P:(blk + 1) * P],
                       w["US"][r:r + 64, blk * P:(blk + 1) * P], False, True).then_inc(st_mm, 1)
                    y_part(w["VTK"], 1, r, blk, c * CH, False)
                    y_part(w["US"], 0, r, blk, c * CH, True)
                    if c < NCH - 1:
                        keys_values(c + 1)
                pe.wait_ge(tatm_ok, i + 1)
                pe.sem_inc(passed, 1)
                u_rest(NCH, 0, BLKS)
                for b in range(NSEQ):
                    last = mm(bank(3, P, 0, 0, 64), w["TATM"][:, b * 64:b * 64 + 64], w["ST0"][:, b * P:(b + 1) * P],
                              False, b == NSEQ - 1)
                last.then_inc(us_mm, 1)
                pe.wait_ge(st_ok, i * 17 + 17)
                pe.wait_ge(usm_ok, i + 1)
                for g in range(2):
                    mm(bank(6 + g), w["BTK"][0:TS, 1024:1152], w["USM"][0:TS, g * 512:(g + 1) * 512], True, False)
                    last = mm(bank(6 + g), w["KTK"][0:TS, 1024:1152], w["VM"][0:TS, g * 512:(g + 1) * 512], False, True)
                for b in range(NSEQ):
                    at = TP + b * LSEQ
                    last = mm(pset(0, at, LSEQ), w["ST0"][:, b * P:(b + 1) * P], w["AR"][:, T + at:T + at + LSEQ],
                              b == 0, False)
                last.then_inc(sst_mm, 1)
                y_part(w["VTK"], 1, 0, BLKS, TP, False)
                y_part(w["US"], 0, 0, BLKS, TP, True).then_inc(y_done, 1)
                warm(3, 5)
                pe.wait_ge(y_ok, i + 1)
                wide(0, headones[:, :], w["YS"]).then_inc(gn_mm, 1)
                pe.wait_ge(sst_ok, i + 1)
                for b in range(NSEQ):
                    pe.transpose(pset(1, b * P, P), w["ST0"][:, b * P:(b + 1) * P], ident[:, :])
                pe.transpose(pset(1, 8 * P, P), state[:, 0:P], ident[:, :]).then_inc(so_tr, 1)
                warm(6, 10)
                pe.wait_ge(gn_act, i * 2 + 1)
                wide(0, headones[:, :], w["SQ"]).then_inc(gn_mm, 1)
                warm(6, 16)
                pe.wait_ge(so_ok, i + 1)
                pe.wait_ge(gn_act, i * 2 + 2)
            pe.wait_ge(rw_out, KT)

            square("rout", xa)
            norm(2)
            mlp(1)
            pe.wait_ge(ple_ct, 2 + 2 * KT)
            for b in range(9):
                n = P if b < BLKS else TS
                if b >= 4:
                    pe.wait_ge(y_rows, b - 3)
                for k in range(KT):
                    last = pe.transpose(bank(b % 4 * 2, P, k * P, 0, n), xs(lo8, k, b * P, n), ident[:, :])
                last.then_inc(y_tr, 1)


INPUTS = ["x_prompt", "x_sample", "cache_k", "cache_v", "state_hgrn", "state_wkv", "state_shift", "page_table",
          "p_prompt", "p_sample", "w_in_even", "w_out_even", "hg_lb_logits", "hg_norm_g",
          "da_lam_q1", "da_lam_k1", "da_lam_q2", "da_lam_k2", "da_norm_g",
          "rw_mix", "rw_w_r", "rw_w_k", "rw_w_v", "rw_w_o", "rw_w0", "rw_w1", "rw_w2",
          "rw_a0", "rw_a1", "rw_a2", "rw_g1", "rw_g2",
          "rw_k_k", "rw_k_a", "rw_r_k", "rw_lnx_g", "rw_lnx_b",
          "ln1_g", "ln1_b", "ln2_g", "ln2_b", "mlp_up", "mlp_down", "ple_proj", "ple_gate"]
OUTPUTS = [("y_prompt", (1, TP, D)), ("y_sample", (NSEQ, LSEQ, D)),
           ("k_prompt", (1, 1, TP, HEADS, 2, 64)), ("v_prompt", (1, 1, TP, HEADS, P)),
           ("k_sample", (1, NSEQ, LSEQ, HEADS, 2, 64)), ("v_sample", (1, NSEQ, LSEQ, HEADS, P)),
           ("hgrn_prompt", (1, 1, HEADS, P, P)), ("hgrn_sample", (1, NSEQ, HEADS, P, P)),
           ("wkv_prompt", (1, 1, 16, 64, 64)), ("wkv_sample", (1, NSEQ, 16, 64, 64)),
           ("shift_prompt", (1, 1, D)), ("shift_sample", (1, NSEQ, D))]


def kernel(**inputs):
    import numpy as _np
    import concourse.bacc as _bacc
    from concourse import mybir as _mybir
    from concourse.bass_utils import run_bass_kernel_spmd as _run

    nc = _bacc.Bacc("TRN2", target_bir_lowering=False, num_devices=1)
    arrays, ins, outs = {}, {}, {}
    for name in INPUTS:
        v = _np.ascontiguousarray(inputs[name])
        arrays["in_" + name] = v
        ins[name] = nc.dram_tensor("in_" + name, v.shape, _mybir.dt.from_np(v.dtype), kind="ExternalInput").ap()
    for name, shape in OUTPUTS:
        outs[name] = nc.dram_tensor("out_" + name, shape, F32, kind="ExternalOutput").ap()
    trunk_program(nc, ins, outs)
    r = _run(nc, [arrays], core_ids=[0])
    return tuple(r.results[0]["out_" + name] for name, _ in OUTPUTS)
```
